# Optimizing a Trainium2 kernel written in Bass

```python
import math
import jax, jax.numpy as jnp
from jax import lax
import numpy as np

D_MODEL = 1024
BATCH = 1
SEQ = 256
DEPTH = 1

HEAD_DIM = 64
DA_HEADS = 4
DA_QK = DA_HEADS * 2 * HEAD_DIM
DA_V = DA_HEADS * 2 * HEAD_DIM
NA_HEADS = 8
NA_W = NA_HEADS * HEAD_DIM
GRID_W = 64
NA_ROWS = 8
NA_COLS = 16
Q_BLOCK = 128
D_FF = int(math.ceil(8 * D_MODEL / 3 / 256) * 256)
IN_COLS = 2 * DA_QK + DA_V + 3 * NA_W + 2 * D_MODEL
EPS = 1e-6
NEG = -1e30


def rmsnorm(x, w):
    xf = x.astype(jnp.float32)
    y = xf * lax.rsqrt(jnp.mean(xf * xf, axis=-1, keepdims=True) + EPS)
    return (y * w.astype(jnp.float32)).astype(x.dtype)

def alibi_slopes(n):
    return jnp.asarray([2.0 ** (-8.0 * (i + 1) / n) for i in range(n)], dtype=jnp.float32)

def diff_attention(q, k, v, lam, subln_w, lambda_init):
    B, S, H, _, d = q.shape
    nb = S // Q_BLOCK
    scale = d ** -0.5
    slopes = alibi_slopes(H)
    kpos = jnp.arange(S)
    qb = jnp.moveaxis(q.reshape(B, nb, Q_BLOCK, H, 2, d), 1, 0)

    def block(args):
        qi, i = args
        s = jnp.einsum('bqhcd,bkhcd->bhcqk', qi, k).astype(jnp.float32) * scale
        qpos = i * Q_BLOCK + jnp.arange(Q_BLOCK)
        dist = jnp.abs(qpos[:, None] - kpos[None, :]).astype(jnp.float32)
        s = s - slopes[None, :, None, None, None] * dist[None, None, None]
        p = jax.nn.softmax(s, axis=-1)
        a = p[:, :, 0] - lam * p[:, :, 1]
        return jnp.einsum('bhqk,bkhe->bqhe', a.astype(v.dtype), v)

    o = lax.map(block, (qb, jnp.arange(nb)))
    o = jnp.moveaxis(o, 0, 1).reshape(B, S, H, 2 * d)
    o = rmsnorm(o, subln_w) * (1.0 - lambda_init)
    return o.reshape(B, S, H * 2 * d)

def neighbourhood_attention_2d(q, k, v, rpb):
    B, S, H, d = q.shape
    rows = S // GRID_W
    kr = min(NA_ROWS, rows)
    kc = NA_COLS
    scale = d ** -0.5
    qg = q.reshape(B, rows, GRID_W, H, d)
    kg = k.reshape(B, rows, GRID_W, H, d)
    vg = v.reshape(B, rows, GRID_W, H, d)
    col = jnp.arange(GRID_W)
    col_start = jnp.clip(col - kc // 2, 0, GRID_W - kc)
    col_in = (col[None, :] >= col_start[:, None]) & (col[None, :] < col_start[:, None] + kc)
    col_off = jnp.clip(col[None, :] - col[:, None] + NA_COLS - 1, 0, 2 * NA_COLS - 2)
    rpb_cols = rpb[:, :, col_off]

    def row_step(args):
        qr, r = args
        rs = jnp.clip(r - kr // 2, 0, rows - kr)
        kb = lax.dynamic_slice_in_dim(kg, rs, kr, axis=1)
        vb = lax.dynamic_slice_in_dim(vg, rs, kr, axis=1)
        s = jnp.einsum('bqhd,bikhd->bhqik', qr, kb).astype(jnp.float32) * scale
        row_off = rs + jnp.arange(kr) - r + NA_ROWS - 1
        bias = jnp.transpose(rpb_cols[:, row_off], (0, 2, 1, 3))
        s = s + bias[None].astype(jnp.float32)
        s = jnp.where(col_in[None, None, :, None, :], s, NEG)
        p = jax.nn.softmax(s, axis=(-2, -1))
        return jnp.einsum('bhqik,bikhd->bqhd', p.astype(v.dtype), vb)

    o = lax.map(row_step, (jnp.moveaxis(qg, 1, 0), jnp.arange(rows)))
    return jnp.moveaxis(o, 0, 1).reshape(B, S, H * d)

def first_inputs(seed: int = 0) -> dict:
    key = jax.random.key(seed)
    ks = jax.random.split(key, 24)
    f32 = jnp.float32

    def nrm(k, shape, scale):
        return jax.random.normal(k, shape, f32) * scale

    def gain(k):
        return 1.0 + nrm(k, (DEPTH, D_MODEL), 0.02)

    return {
        "x": nrm(ks[0], (BATCH, SEQ, D_MODEL), 1.0),
        "pre_mix_w": gain(ks[1]),
        "w_in": nrm(ks[2], (DEPTH, D_MODEL, IN_COLS), D_MODEL ** -0.5),
        "b_gate": nrm(ks[3], (DEPTH, 2 * D_MODEL), 0.1),
        "lambda_q1": nrm(ks[4], (DEPTH, HEAD_DIM), 0.1),
        "lambda_k1": nrm(ks[5], (DEPTH, HEAD_DIM), 0.1),
        "lambda_q2": nrm(ks[6], (DEPTH, HEAD_DIM), 0.1),
        "lambda_k2": nrm(ks[7], (DEPTH, HEAD_DIM), 0.1),
        "subln_w": 1.0 + nrm(ks[8], (DEPTH, 2 * HEAD_DIM), 0.02),
        "rpb": nrm(ks[9], (DEPTH, NA_HEADS, 2 * NA_ROWS - 1, 2 * NA_COLS - 1), 0.1),
        "w_branch_a": nrm(ks[10], (DEPTH, DA_V, D_MODEL), DA_V ** -0.5),
        "w_branch_b": nrm(ks[11], (DEPTH, NA_W, D_MODEL), NA_W ** -0.5),
        "w_out": nrm(ks[12], (DEPTH, D_MODEL, D_MODEL), D_MODEL ** -0.5),
        "post_mix_w": gain(ks[13]),
        "pre_ffn_w": gain(ks[14]),
        "w_gate": nrm(ks[15], (DEPTH, D_MODEL, D_FF), D_MODEL ** -0.5),
        "w_up": nrm(ks[16], (DEPTH, D_MODEL, D_FF), D_MODEL ** -0.5),
        "w_down": nrm(ks[17], (DEPTH, D_FF, D_MODEL), D_FF ** -0.5),
        "post_ffn_w": gain(ks[18]),
    }

def first_block(x, pre_mix_w, w_in, b_gate, lambda_q1, lambda_k1, lambda_q2, lambda_k2,
              subln_w, rpb, w_branch_a, w_branch_b, w_out, post_mix_w, pre_ffn_w,
              w_gate, w_up, w_down, post_ffn_w):
    B, S, _ = x.shape
    for l in range(DEPTH):
        lambda_init = 0.8 - 0.6 * math.exp(-0.3 * l)
        h = rmsnorm(x, pre_mix_w[l])
        proj = h @ w_in[l]
        o0 = 0
        q_a = proj[..., o0:o0 + DA_QK].reshape(B, S, DA_HEADS, 2, HEAD_DIM); o0 += DA_QK
        k_a = proj[..., o0:o0 + DA_QK].reshape(B, S, DA_HEADS, 2, HEAD_DIM); o0 += DA_QK
        v_a = proj[..., o0:o0 + DA_V].reshape(B, S, DA_HEADS, 2 * HEAD_DIM); o0 += DA_V
        q_b = proj[..., o0:o0 + NA_W].reshape(B, S, NA_HEADS, HEAD_DIM); o0 += NA_W
        k_b = proj[..., o0:o0 + NA_W].reshape(B, S, NA_HEADS, HEAD_DIM); o0 += NA_W
        v_b = proj[..., o0:o0 + NA_W].reshape(B, S, NA_HEADS, HEAD_DIM); o0 += NA_W
        gates = jax.nn.sigmoid(proj[..., o0:] + b_gate[l])
        g_a, g_b = gates[..., :D_MODEL], gates[..., D_MODEL:]

        lq1 = lambda_q1[l].astype(jnp.float32); lk1 = lambda_k1[l].astype(jnp.float32)
        lq2 = lambda_q2[l].astype(jnp.float32); lk2 = lambda_k2[l].astype(jnp.float32)
        lam = jnp.exp(jnp.sum(lq1 * lk1)) - jnp.exp(jnp.sum(lq2 * lk2)) + lambda_init

        y_a = diff_attention(q_a, k_a, v_a, lam, subln_w[l], lambda_init)
        y_b = neighbourhood_attention_2d(q_b, k_b, v_b, rpb[l])
        merged = g_a * (y_a @ w_branch_a[l]) + g_b * (y_b @ w_branch_b[l])
        x = x + rmsnorm(merged @ w_out[l], post_mix_w[l])
        h = rmsnorm(x, pre_ffn_w[l])
        f = (jax.nn.silu(h @ w_gate[l]) * (h @ w_up[l])) @ w_down[l]
        x = x + rmsnorm(f, post_ffn_w[l])
    return x


MLA_HEADS = 8
MLA_NOPE_DIM = 64
MLA_ROPE_DIM = 32
MLA_QK_DIM = MLA_NOPE_DIM + MLA_ROPE_DIM
MLA_V_DIM = 64
MLA_WIDTH = MLA_HEADS * MLA_V_DIM
MLA_Q_RANK = 384
MLA_KV_RANK = 256
ROPE_THETA = 10000.0
GLA_HEADS = 4
GLA_DV = D_MODEL // 2
GLA_DK = GLA_DV // 2
GLA_HEAD_K = GLA_DK // GLA_HEADS
GLA_HEAD_V = GLA_DV // GLA_HEADS
GLA_GATE_RANK = 16
GLA_GATE_TAU = 16.0
GLA_CHUNK = 64
D_FF_2 = -(-8 * D_MODEL // (3 * 256)) * 256
NORM_EPS = 1e-6
IN_SIZES = (MLA_Q_RANK, MLA_KV_RANK, MLA_ROPE_DIM,
            GLA_DK, GLA_DK, GLA_DV, GLA_GATE_RANK, GLA_DV,
            D_MODEL, D_MODEL)
D_IN = sum(IN_SIZES)


def rmsnorm_2(x, w):
    xf = x.astype(jnp.float32)
    y = xf * lax.rsqrt(jnp.mean(xf * xf, axis=-1, keepdims=True) + NORM_EPS)
    return (y * w.astype(jnp.float32)).astype(x.dtype)

def rope_tables(positions):
    half = MLA_ROPE_DIM // 2
    inv = 1.0 / (ROPE_THETA ** (jnp.arange(half, dtype=jnp.float32) / half))
    ang = positions.astype(jnp.float32)[..., None] * inv
    return jnp.cos(ang), jnp.sin(ang)

def apply_rope(x, cos, sin):
    x1, x2 = jnp.split(x.astype(jnp.float32), 2, axis=-1)
    return jnp.concatenate([x1 * cos - x2 * sin, x2 * cos + x1 * sin], axis=-1).astype(x.dtype)

def mla(c_q, c_kv, k_rope, cos, sin, norm_cq, w_uq, norm_ckv, w_ukv):
    B, S, _ = c_q.shape
    H = MLA_HEADS
    q = (rmsnorm_2(c_q, norm_cq) @ w_uq).reshape(B, S, H, MLA_QK_DIM)
    q_nope, q_rope = q[..., :MLA_NOPE_DIM], q[..., MLA_NOPE_DIM:]
    q_rope = apply_rope(q_rope, cos[:, :, None], sin[:, :, None])
    kv = (rmsnorm_2(c_kv, norm_ckv) @ w_ukv).reshape(B, S, H, MLA_NOPE_DIM + MLA_V_DIM)
    k_nope, v = kv[..., :MLA_NOPE_DIM], kv[..., MLA_NOPE_DIM:]
    k_rope = apply_rope(k_rope, cos, sin)
    k = jnp.concatenate([k_nope, jnp.broadcast_to(k_rope[:, :, None], (B, S, H, MLA_ROPE_DIM)).astype(k_nope.dtype)], axis=-1)
    q = jnp.concatenate([q_nope, q_rope], axis=-1) * (MLA_QK_DIM ** -0.5)
    nb = S // Q_BLOCK
    q_blocks = q.reshape(B, nb, Q_BLOCK, H, MLA_QK_DIM).transpose(1, 0, 2, 3, 4)
    key_idx = jnp.arange(S)

    def attend(args):
        q_blk, start = args
        s = jnp.einsum('bqhd,bkhd->bhqk', q_blk, k).astype(jnp.float32)
        q_idx = start + jnp.arange(Q_BLOCK)
        mask = key_idx[None, :] <= q_idx[:, None]
        s = jnp.where(mask, s, -jnp.inf)
        p = jax.nn.softmax(s, axis=-1).astype(v.dtype)
        return jnp.einsum('bhqk,bkhd->bqhd', p, v)

    o = lax.map(attend, (q_blocks, jnp.arange(nb) * Q_BLOCK))
    return o.transpose(1, 0, 2, 3, 4).reshape(B, S, MLA_WIDTH)

def gla(q, k, v, g_lr, og, w_gate2, b_gate, norm_o):
    B, S, _ = q.shape
    H, C = GLA_HEADS, GLA_CHUNK
    n = S // C
    log_a = jax.nn.log_sigmoid((g_lr @ w_gate2 + b_gate).astype(jnp.float32)) / GLA_GATE_TAU

    def heads(t, d):
        return t.reshape(B, S, H, d).transpose(0, 2, 1, 3).astype(jnp.float32)

    def chunks(t):
        return t.reshape(B, H, n, C, t.shape[-1]).transpose(2, 0, 1, 3, 4)

    qh = heads(q, GLA_HEAD_K) * (GLA_HEAD_K ** -0.5)
    kh = heads(k, GLA_HEAD_K)
    vh = heads(v, GLA_HEAD_V)
    gh = heads(log_a, GLA_HEAD_K)
    bcum = jnp.cumsum(chunks(gh), axis=3)
    causal = jnp.tril(jnp.ones((C, C), dtype=bool))

    def step(state, xs):
        qc, kc, vc, bc = xs
        o_inter = jnp.einsum('bhcd,bhde->bhce', qc * jnp.exp(bc), state)
        diff = bc[:, :, :, None, :] - bc[:, :, None, :, :]
        decay = jnp.exp(jnp.where(causal[:, :, None], diff, -jnp.inf))
        attn = jnp.einsum('bhid,bhjd,bhijd->bhij', qc, kc, decay)
        o_intra = jnp.einsum('bhij,bhje->bhie', attn, vc)
        b_last = bc[:, :, -1:, :]
        k_dec = kc * jnp.exp(b_last - bc)
        state = jnp.exp(b_last[:, :, 0, :])[..., None] * state + jnp.einsum('bhcd,bhce->bhde', k_dec, vc)
        return state, o_inter + o_intra

    state0 = jnp.zeros((B, H, GLA_HEAD_K, GLA_HEAD_V), jnp.float32)
    _, o = lax.scan(step, state0, (chunks(qh), chunks(kh), chunks(vh), bcum))
    o = o.transpose(1, 0, 3, 2, 4).reshape(B, S, H, GLA_HEAD_V)
    o = rmsnorm_2(o, norm_o).reshape(B, S, GLA_DV)
    o = o * jax.nn.silu(og.astype(jnp.float32))
    return o.astype(q.dtype)

def second_inputs(seed: int = 0) -> dict:
    key = jax.random.key(seed)
    ks = jax.random.split(key, 24)
    L, D = DEPTH, D_MODEL

    def w(k, shape, fan_in):
        return jax.random.normal(k, shape, jnp.float32) * (fan_in ** -0.5)

    def gain(k, shape):
        return 1.0 + 0.02 * jax.random.normal(k, shape, jnp.float32)

    return {
        "x": jax.random.normal(ks[0], (BATCH, SEQ, D), jnp.float32),
        "positions": jnp.broadcast_to(jnp.arange(SEQ, dtype=jnp.int32), (BATCH, SEQ)),
        "ln_mix": gain(ks[1], (L, D)),
        "w_in": w(ks[2], (L, D, D_IN), D),
        "mla_norm_cq": gain(ks[3], (L, MLA_Q_RANK)),
        "mla_w_uq": w(ks[4], (L, MLA_Q_RANK, MLA_HEADS * MLA_QK_DIM), MLA_Q_RANK),
        "mla_norm_ckv": gain(ks[5], (L, MLA_KV_RANK)),
        "mla_w_ukv": w(ks[6], (L, MLA_KV_RANK, MLA_HEADS * (MLA_NOPE_DIM + MLA_V_DIM)), MLA_KV_RANK),
        "mla_w_o": w(ks[7], (L, MLA_WIDTH, D), MLA_WIDTH),
        "gla_w_gate2": w(ks[8], (L, GLA_GATE_RANK, GLA_DK), GLA_GATE_RANK),
        "gla_b_gate": 0.1 * jax.random.normal(ks[9], (L, GLA_DK), jnp.float32),
        "gla_norm": gain(ks[10], (L, GLA_HEAD_V)),
        "gla_w_o": w(ks[11], (L, GLA_DV, D), GLA_DV),
        "w_out": w(ks[12], (L, D, D), D),
        "ln_ffn": gain(ks[13], (L, D)),
        "ffn_w_gate": w(ks[14], (L, D, D_FF_2), D),
        "ffn_w_up": w(ks[15], (L, D, D_FF_2), D),
        "ffn_w_down": w(ks[16], (L, D_FF_2, D), D_FF_2),
        "final_norm": gain(ks[17], (D,)),
    }

def second_block(x, positions, ln_mix, w_in, mla_norm_cq, mla_w_uq, mla_norm_ckv, mla_w_ukv, mla_w_o,
              gla_w_gate2, gla_b_gate, gla_norm, gla_w_o, w_out, ln_ffn, ffn_w_gate, ffn_w_up,
              ffn_w_down, final_norm):
    offsets = np.cumsum(IN_SIZES)[:-1].tolist()
    cos, sin = rope_tables(positions)
    h = x
    for l in range(DEPTH):
        u = rmsnorm_2(h, ln_mix[l])
        z = u @ w_in[l]
        c_q, c_kv, k_rope, g_q, g_k, g_v, g_lr, g_og, gate_a, gate_b = jnp.split(z, offsets, axis=-1)
        y_a = mla(c_q, c_kv, k_rope, cos, sin, mla_norm_cq[l], mla_w_uq[l], mla_norm_ckv[l], mla_w_ukv[l]) @ mla_w_o[l]
        y_b = gla(g_q, g_k, g_v, g_lr, g_og, gla_w_gate2[l], gla_b_gate[l], gla_norm[l]) @ gla_w_o[l]
        mix = jax.nn.sigmoid(gate_a) * y_a + jax.nn.sigmoid(gate_b) * y_b
        h = h + mix @ w_out[l]
        u = rmsnorm_2(h, ln_ffn[l])
        h = h + (jax.nn.silu(u @ ffn_w_gate[l]) * (u @ ffn_w_up[l])) @ ffn_w_down[l]
    return rmsnorm_2(h, final_norm)


def setup_inputs(seed=0):
    out = dict(first_inputs(seed))
    for name, value in second_inputs(seed + 1).items():
        if name != "x":
            out[name + "_2"] = value
    return out


def reference(
    x, pre_mix_w, w_in, b_gate, lambda_q1, lambda_k1, lambda_q2, lambda_k2, subln_w, rpb,
    w_branch_a, w_branch_b, w_out, post_mix_w, pre_ffn_w, w_gate, w_up, w_down, post_ffn_w,
    positions_2, ln_mix_2, w_in_2, mla_norm_cq_2, mla_w_uq_2, mla_norm_ckv_2, mla_w_ukv_2,
    mla_w_o_2, gla_w_gate2_2, gla_b_gate_2, gla_norm_2, gla_w_o_2, w_out_2, ln_ffn_2,
    ffn_w_gate_2, ffn_w_up_2, ffn_w_down_2, final_norm_2,
):
    x = first_block(
        x, pre_mix_w, w_in, b_gate, lambda_q1, lambda_k1, lambda_q2, lambda_k2, subln_w, rpb,
        w_branch_a, w_branch_b, w_out, post_mix_w, pre_ffn_w, w_gate, w_up, w_down, post_ffn_w,
    )
    return second_block(
        x, positions_2, ln_mix_2, w_in_2, mla_norm_cq_2, mla_w_uq_2, mla_norm_ckv_2,
        mla_w_ukv_2, mla_w_o_2, gla_w_gate2_2, gla_b_gate_2, gla_norm_2, gla_w_o_2, w_out_2,
        ln_ffn_2, ffn_w_gate_2, ffn_w_up_2, ffn_w_down_2, final_norm_2,
    )


_drawn_inputs = setup_inputs


def setup_inputs(seed=0):
    import zlib

    import numpy as np

    out = dict(_drawn_inputs(seed))
    spreads = {}
    factors = {'subln_w': 3.056,
     'rpb': 2.714,
     'post_mix_w': 2.982,
     'pre_ffn_w': 3.124,
     'post_ffn_w': 4.538,
     'ln_mix_2': 6.456,
     'mla_norm_cq_2': 8.0,
     'mla_norm_ckv_2': 8.0,
     'gla_b_gate_2': 6.942,
     'gla_norm_2': 8.0,
     'ln_ffn_2': 16.566,
     'final_norm_2': 8.075}
    for name, (base, spread) in spreads.items():
        noise = np.random.default_rng([zlib.crc32(name.encode()), seed]).standard_normal(out[name].shape)
        drawn = base * np.exp(spread * noise) if base else spread * noise
        out[name] = __import__('jax').numpy.asarray(drawn.astype(out[name].dtype))
    for name, factor in factors.items():
        out[name] = (out[name] * factor).astype(out[name].dtype)
    return out
```

```python
import math
from contextlib import ExitStack

import concourse.bass as bass
from concourse import mybir

F32 = mybir.dt.float32
F32R = mybir.dt.float32r
I32 = mybir.dt.int32
U32 = mybir.dt.uint32
ALU = mybir.AluOpType
ACT = mybir.ActivationFunctionType
AX = mybir.AxisListType

P = 128
SEQ = 256
TOKS = SEQ // P
D = 1024
KD = D // P
D_FF = 2816
KF = D_FF // P
EPS = 1e-6
FAR = 1e30
BIG = 3e38

DA_HEADS, NA_HEADS, HD = 4, 8, 64
GRID, NA_ROWS, NA_COLS = 64, 8, 16
RPB_ROW, RPB_HEAD = 2 * NA_COLS - 1, (2 * NA_ROWS - 1) * (2 * NA_COLS - 1)
MLA_H, NOPE, ROPE, MLA_QK, MLA_V = 8, 64, 32, 96, 64
Q_RANK, KV_RANK = 384, 256
GLA_H, GLA_DK, GLA_DV, GLA_CHUNK = 4, 64, 128, 64
LEVELS = (32, 16, 8, 4, 2, 1)

RING = 9
LAG = 3

SUPER = [
    ("qk_a", ("w_in",), KD, ((0, 0, 512, 0), (0, 512, 512, 512))),
    ("v_a_q_b", ("w_in",), KD, ((0, 1024, 512, 0), (0, 1536, 512, 512))),
    ("k_b_v_b", ("w_in",), KD, ((0, 2048, 512, 0), (0, 2560, 512, 512))),
    ("gate_a", ("w_in",), KD, ((0, 3072, 512, 0), (0, 3584, 512, 512))),
    ("gate_b", ("w_in",), KD, ((0, 4096, 512, 0), (0, 4608, 512, 512))),
    ("branch_a", ("w_branch_a",), 4, ((0, 0, 512, 0), (0, 512, 512, 512))),
    ("branch_b", ("w_branch_b",), 4, ((0, 0, 512, 0), (0, 512, 512, 512))),
    ("out", ("w_out",), KD, ((0, 0, 512, 0), (0, 512, 512, 512))),
    *[(f"up{j}", ("w_gate", "w_up"), KD, ((0, 512 * j, 512, 0), (1, 512 * j, 512, 512))) for j in range(5)],
    ("up5", ("w_gate", "w_up"), KD, ((0, 2560, 256, 0), (1, 2560, 256, 256))),
    ("down", ("w_down",), KF, ((0, 0, 512, 0), (0, 512, 512, 512))),
    ("latent", ("w_in_2",), KD, ((0, 0, 384, 0), (0, 384, 288, 384))),
    ("gla_qkv", ("w_in_2",), KD, ((0, 672, 512, 0), (0, 1184, 512, 512))),
    ("gla_og", ("w_in_2",), KD, ((0, 1712, 512, 16), (0, 1696, 16, 0))),
    ("gate_a2", ("w_in_2",), KD, ((0, 2224, 512, 0), (0, 2736, 512, 512))),
    ("uq", ("mla_w_uq_2",), 3, ((0, 0, 384, 0), (0, 384, 384, 384))),
    ("ukv", ("mla_w_ukv_2",), 2, ((0, 0, 512, 0), (0, 512, 512, 512))),
    ("gate_b2", ("w_in_2",), KD, ((0, 3248, 512, 0), (0, 3760, 512, 512))),
    ("gla_o", ("gla_w_o_2",), 4, ((0, 0, 512, 0), (0, 512, 512, 512))),
    ("mla_o", ("mla_w_o_2",), 4, ((0, 0, 512, 0), (0, 512, 512, 512))),
    ("out2", ("w_out_2",), KD, ((0, 0, 512, 0), (0, 512, 512, 512))),
    *[(f"up2{j}", ("ffn_w_gate_2", "ffn_w_up_2"), KD, ((0, 512 * j, 512, 0), (1, 512 * j, 512, 512)))
      for j in range(5)],
    ("up25", ("ffn_w_gate_2", "ffn_w_up_2"), KD, ((0, 2560, 256, 0), (1, 2560, 256, 256))),
    ("down2", ("ffn_w_down_2",), KF, ((0, 0, 512, 0), (0, 512, 512, 512))),
]
SC = {s[0]: s for s in SUPER}
FIRST, UNITS = {}, []
for _s in SUPER:
    FIRST[_s[0]] = len(UNITS)
    UNITS += [(_s[0], kt) for kt in range(_s[2])]




def timeline(last=None):
    out = []

    def do(*step):
        return ("do",) + step

    def mm(name, group, tasks=(), lead=0, every=1):
        n = SC[name][2]
        items = [("mm", name, t, kt) for g in range(0, n, group) for t in range(TOKS)
                 for kt in range(g, min(g + group, n))]
        left = list(tasks)
        for i, it in enumerate(items):
            out.append(it)
            if it[3] == n - 1:
                out.append(("take", name, it[2]))
            if left and i >= lead and (i - lead) % every == 0:
                out.extend(left.pop(0))
        for rest in left:
            out.extend(rest)

    def whole(name, t, inside=None, behind=6):
        for kt in range(SC[name][2]):
            out.append(("mm", name, t, kt))
            if inside and kt == behind:
                out.append(inside)
        out.append(("take", name, t))

    def ffn(up, down, tag, nxt):
        whole(f"{up}0", 0, do("norm_turn", tag, 1), 6)
        whole(f"{up}0", 1, do("ffn_turn", f"{up}0", 0), 4)
        for j in range(1, 5):
            name = f"{up}{j}"
            mm(name, 4, [[do("ffn_turn", f"{up}{j - 1}", 1)], [do("ffn_turn", name, 0)]], 4, 11)
        whole(f"{up}5", 0, do("ffn_turn", f"{up}4", 1), 4)
        whole(f"{up}5", 1, do("ffn_turn", f"{up}5", 0), 6)
        tail = KF - KD
        for g in range(0, tail, 4):
            for t in range(TOKS):
                for kt in range(g, min(g + 4, tail)):
                    out.append(("mm", down, t, kt))
                    if (t, kt) == (0, 3):
                        out.append(do("ffn_turn", f"{up}5", 1))
        for t in range(TOKS):
            for kt in range(tail, KF):
                out.append(("mm", down, t, kt))
                if nxt and (t, kt) == (1, KF - 2):
                    out.append(do("norm_turn", nxt, 0))
            if nxt and t == 1:
                out.append(("ahead", FIRST[down] + KF + 5))
            out.append(("take", down, t))

    out.append(do("first_norm", 0))
    out.append(("ahead", 1))
    out.append(do("norm_turn", "mix", 0))
    out.append(do("first_norm", 1))
    whole("qk_a", 0, do("norm_turn", "mix", 1), 3)
    whole("qk_a", 1, do("setup"), 1)
    mm("v_a_q_b", 2, [[do("qk_a_turn", 0)], [do("qk_a_turn", 1)]], 1, 4)
    q = [[] for _ in range(24)]
    q[0].append(do("q_b_turn", 0))
    q[1].append(do("q_b_turn", 1))
    q[9].append(do("k_b_turn", 0))
    q[10].append(do("k_b_turn", 1))
    for i in range(8):
        q[i].append(do("score", "da", i))
        q[i + 1].append(do("combine", i))
        q[i + 2].append(do("turn_p", "da", i))
        q[i + 3].append(do("pv", "da", i))
        if i % 4 == 3:
            q[i + 4].append(do("da_norm", i // 4))
            q[i + 5].append(do("da_heads", i // 4))
            q[i + 6].append(do("turn_y", "da", i // 4))
    for i in range(8):
        q[10 + i].append(do("score", "na", i))
        q[12 + i].append(do("turn_p", "na", i))
        q[13 + i].append(do("pv", "na", i))
        if i % 4 == 3:
            q[14 + i].append(do("head_norm", "na", i // 4))
            q[15 + i].append(do("turn_y", "na", i // 4))
    FIRST_OF = ("da_norm", "head_norm", "score", "pv", "turn_p", "combine", "da_heads", "turn_y")
    order = lambda slot: sorted(slot, key=lambda st: FIRST_OF.index(st[1]) if st[1] in FIRST_OF else -1)
    q = [order(slot) for slot in q]
    mm("k_b_v_b", 1, q[0:8], 1, 2)
    mm("gate_a", 1, q[8:16], 1, 2)
    mm("gate_b", 1, q[16:24], 1, 2)
    mm("branch_a", 4)
    whole("branch_b", 0)
    whole("branch_b", 1, do("norm_turn", "merged", 0), 2)
    whole("out", 0, do("norm_turn", "merged", 1), 3)
    whole("out", 1, do("norm_turn", "ffn", 0), 6)
    ffn("up", "down", "ffn", None if last == 1 else "mix2")
    if last == 1:
        return out
    whole("latent", 0, do("norm_turn", "mix2", 1), 6)
    whole("latent", 1)
    mm("gla_qkv", 4, [[do("latent_turn", 0)], [do("latent_turn", 1)]], 4, 4)
    mm("gla_og", 4, [[do("gla_qk_turn", 0)], [do("gla_qk_turn", 1)]], 4, 4)
    g = [[] for _ in range(13)]
    g[0] = [do("gate_lr_turn", 0)]
    g[1] = [do("gate_lr_turn", 1)]
    g[2] = [do("decay_logits")]
    g[4] = [do("decay_sums")]
    for n in range(len(LEVELS)):
        g[5 + n].append(do("gla_decay", n))
        g[6 + n].append(do("gla_level", n + 1))
    g[5].append(do("gla_level", 0))
    for n in range(len(LEVELS)):
        g[5 + n].append(do("gla_keys", n))
    g[12].append(do("gla_state"))
    mm("gate_a2", 1, g[0:8], 1, 2)
    mm("uq", 1, g[8:11], 1, 2)
    mm("ukv", 1, g[11:13], 1, 2)
    m = [[] for _ in range(16)]
    m[0] = [do("gla_output", 0), do("gla_output", 1)]
    m[1] = [do("mla_turn", 0)]
    m[2] = [do("mla_turn", 1), do("turn_y", "gla", 0)]
    m[3] = [do("turn_y", "gla", 1)]
    for i in range(8):
        m[i + 3].append(do("score", "mla", i))
        m[i + 5].append(do("turn_p", "mla", i))
        m[i + 6].append(do("pv", "mla", i))
        if i % 4 == 3:
            m[i + 7].append(do("head_norm", "mla", i // 4))
            m[i + 8].append(do("turn_y", "mla", i // 4))
    m = m[0:3] + [order(slot) for slot in m[3:]]
    mm("gate_b2", 1, m[0:8], 1, 2)
    mm("gla_o", 1, m[8:16], 0, 1)
    whole("mla_o", 0)
    whole("mla_o", 1, do("norm_turn", "merged2", 0), 2)
    whole("out2", 0, do("norm_turn", "merged2", 1), 3)
    whole("out2", 1, do("norm_turn", "ffn2", 0), 6)
    ffn("up2", "down2", "ffn2", None)
    return out


def program(nc, known, last, ins, out):
    marks, counts, sems = {}, {}, {}
    steps = timeline(last)
    ctx = ExitStack()
    with ctx:
        def tick(name, key=None, by=1):
            if name not in sems:
                sems[name] = ctx.enter_context(nc.semaphore(name))
            counts[name] = counts.get(name, 0) + by
            marks[name, key] = counts[name]
            return sems[name], by

        def at(name, key=None):
            if name not in sems:
                sems[name] = ctx.enter_context(nc.semaphore(name))
            return sems[name], known.get((name, key), 1) if known else 1

        def last_of(name):
            return sems[name], counts[name]

        def sb(name, shape, dtype=F32, scope=ctx):
            return scope.enter_context(nc.sbuf_tensor(name, shape, dtype))

        hi = sb("weights_high", [P, RING, 1024], F32R)
        with ExitStack() as s:
            raw = sb("weights_raw", [P, RING, 1024], F32, s)
        lo = sb("weights_low", [P, RING, 1024], F32R)
        row = sb("row", [P, TOKS, D])
        hT = [sb("h_high", [P, KD, SEQ], F32R), sb("h_low", [P, KD, SEQ], F32R)]
        yT = [sb("y_high", [P, KD, SEQ], F32R), sb("y_low", [P, KD, SEQ], F32R)]
        gain = sb("gain", [P, 2, D])
        ident = sb("ident", [P, P])
        stats = sb("stats", [P, 256])
        half = sb("minus_half", [P, 4])
        lam = sb("lambda", [P, 4])
        pos_i = sb("positions", [P, TOKS], I32)
        pos_f = sb("positions_f", [P, TOKS])
        inv = sb("inverse_period", [P, 16])
        angle = sb("angle", [P, TOKS, 16])
        turns = sb("turns", [P, TOKS, 16])
        cos2 = sb("cosine", [P, TOKS, 2, 16])
        sin = sb("sine", [P, TOKS, 16])
        causal = sb("causal", [P, SEQ])
        upto = sb("sum_up_to", [P, P])
        after = sb("sum_after", [P, P])
        lmask = sb("level_mask", [P, 7, GLA_CHUNK])

        def sb1(name, shape, dtype=F32):
            return sb(name, shape, dtype, att1)

        with ExitStack() as att1:
            qaT = sb1("q_a_T", [P, 2, DA_HEADS, SEQ])
            kaT = sb1("k_a_T", [P, DA_HEADS, SEQ])
            va = sb1("v_a", [P, TOKS, 512])
            qbT = sb1("q_b_T", [P, 2, 4, SEQ])
            kbT = sb1("k_b_T", [P, 4, SEQ])
            vb = sb1("v_b", [P, TOKS, 512])
            T1 = sb1("probs_1", [P, 2, 512])
            PT1 = sb1("probs_T_1", [P, 2, 512])
            ob1 = sb1("heads_1", [P, 512])
            gates1 = sb1("gates_1", [P, 2, TOKS, D])
            lam_in = sb1("lambda_in", [P, 4, HD])
            sub_w = sb1("subln_bc", [P, P])
            dist = sb1("distance", [P, TOKS, SEQ])
            nbias = sb1("minus_bias", [P, NA_HEADS, 6, GRID])
        x = sb("x", [P, TOKS, D])
        with ExitStack() as s:
            gqk = sb("gla_qk", [P, TOKS, 512], F32, s)
            gv = sb("gla_v", [P, TOKS, 512], F32, s)
            gqT = sb("gla_q_T", [P, 2, SEQ], F32, s)
            gkT = sb("gla_k_T", [P, 2, SEQ], F32, s)
            gl = sb("log_decay", [P, TOKS, 256], F32, s)
            bT = sb("decay_sum_T", [P, 2, SEQ], F32, s)
            kdec = sb("k_decayed", [P, TOKS, 256], F32, s)
            qdec = sb("q_decayed_T", [P, 2, 2, SEQ], F32, s)
            ED = sb("level_decay", [P, 512], F32, s)
            QE = sb("level_q", [P, 2, SEQ], F32, s)
            gz, KE = QE, gl
            AC = sb("gla_attn_parts", [P, 2, 4, GLA_CHUNK], F32, s)
            AT = sb("gla_attn_T", [P, TOKS, 2, 2, 2, GLA_CHUNK], F32, s)
            dchunk = sb("chunk_decay", [P, 2, 4], F32, s)
            ST = sb("gla_states", [P, 3, 2, GLA_DV], F32, s)
        with ExitStack() as s:
            gb2 = sb("gates_b2", [P, TOKS, D], F32, s)
            qmT = sb("q_latent_T", [MLA_QK, MLA_H, SEQ], F32, s)
            kmT = sb("k_latent_T", [MLA_QK, MLA_H, SEQ], F32, s)
            T2 = sb("probs_2", [P, 2, 512], F32, s)
            PT2 = sb("probs_T_2", [P, 2, 512], F32, s)
        with ExitStack() as s:
            fT = [sb("f_high", [P, KF - KD, SEQ], F32R, s), sb("f_low", [P, KF - KD, SEQ], F32R, s)]
            fe = sb("silu_tmp", [P, TOKS, 512], F32, s)
        with ExitStack() as s:
            sb("three_groups", [P, 9000], F32, s)
            ga2 = sb("gates_a2", [P, TOKS, D], F32, s)
            sil = sb("silu_og", [P, TOKS, 512], F32, s)
            lr = sb("gate_lr", [P, TOKS, 16], F32, s)
            lrT = sb("gate_lr_T", [16, SEQ], F32, s)
            ktm = sb("k_latent", [P, TOKS, MLA_H, MLA_QK], F32, s)
            vm = sb("v_latent", [P, TOKS, 512], F32, s)
            kr = sb("k_rope", [P, TOKS, 2, 16], F32, s)
            rt = sb("rope_tmp", [P, 2, MLA_H, 2, 16], F32, s)
            ob2 = sb("heads_2", [P, TOKS, 512], F32, s)
            cq_w = sb("norm_cq_bc", [P, Q_RANK], F32, s)
            ckv_w = sb("norm_ckv_bc", [P, KV_RANK], F32, s)
            gln_w = sb("gla_norm_bc", [P, GLA_DV], F32, s)
            gb_w = sb("gla_bias_bc", [P, 256], F32, s)
            wg2 = sb("gla_gate2", [16, 256], F32, s)

        acc = ctx.enter_context(nc.psum_tensor("acc", [P, 4, 512], F32))
        aux = [ctx.enter_context(nc.psum_tensor(f"aux{i}", [P, 512], F32)) for i in range(4)]

        def acc_of(t):
            return acc[:, 2 * t:2 * t + 2, :]

        free_col = [0]
        cols = {}

        def stat(key, n=1):
            if key not in cols:
                cols[key] = free_col[0]
                free_col[0] += n
                assert free_col[0] <= 256
            return stats[:, cols[key]:cols[key] + n]

        def operand(name, kt):
            if name in ("branch_a", "mla_o"):
                return yT, kt
            if name in ("branch_b", "gla_o"):
                return yT, 4 + kt
            if name == "uq":
                return yT, kt
            if name == "ukv":
                return yT, 3 + kt
            if name in ("down", "down2"):
                return (yT, kt) if kt < KD else (fT, kt - KD)
            return hT, kt

        OPERAND_READY = {"qk_a": "mix", "branch_a": "y_da", "branch_b": "y_na", "out": "merged", "up0": "ffn",
                         "latent": "mix2", "uq": "latent", "ukv": "latent", "gla_o": "y_gla", "mla_o": "y_mla",
                         "out2": "merged2", "up20": "ffn2"}
        used_before, n_used = [], 0
        for st in steps:
            used_before.append(n_used)
            if st[0] == "mm" and st[2] == TOKS - 1:
                n_used += 1
        n_units = n_used

        def ahead_of(i):
            _, name, _, kt = steps[i]
            return max(used_before[i] + RING - LAG, FIRST[name] + kt + 2)

        names = [s_[0] for s_ in SUPER if FIRST[s_[0]] < n_units]

        def slot_free(u):
            name, kt = UNITS[u]
            return ("mm_done", (name, TOKS - 1)) if kt == SC[name][2] - 1 else ("weights_used", u)

        def unit_width(name):
            return sum(p_[2] for p_ in SC[name][3])

        def att_q(kind, hb, i):
            qt, n = divmod(i, 4)
            s_ = slice(qt * P, qt * P + P)
            if kind == "mla":
                return qmT[:, 2 * n + hb, s_]
            return (qaT if kind == "da" else qbT)[:, hb, n, s_]

        def att_k(kind, hb, i):
            qt, n = divmod(i, 4)
            if kind == "mla":
                return kmT[:, 2 * n + hb, 0:(qt + 1) * P]
            return (kaT if kind == "da" else kbT)[:, n, :]

        def att_keys(kind, i):
            return (i // 4 + 1) * P if kind == "mla" else SEQ

        probs = {"da": T1, "na": T1, "mla": T2}
        probs_T = {"da": PT1, "na": PT1, "mla": PT2}

        block = ctx.enter_context(nc.Block())

        @block.sync
        def _(sp):
            dram = ins

            def load_x(t):
                sp.dma_start(x[:, t, :], dram["x"][0, t * P:(t + 1) * P, :]).then_inc(*tick(f"x_loaded{t}", None, 16))

            def bc(ap, n=P):
                return ap.to_broadcast([n, ap.shape[-1]]) if ap.shape[0] == 1 else ap

            def load_small(dst, src, key):
                sp.dma_start(dst, src).then_inc(*tick("small_loaded", key, 16))

            def weights(u):
                name, kt = UNITS[u]
                slot = u % RING
                if u >= RING:
                    sp.wait_ge(*at(*slot_free(u - RING)))
                for m, c, w, d in SC[name][3]:
                    src = dram[SC[name][1][m]][0, kt * P:(kt + 1) * P, c:c + w]
                    sp.dma_start(raw[:, slot, d:d + w], src).then_inc(*tick(f"raw_loaded{slot}", u, 16))

            load_x(0)
            sp.dma_start(gain[:, 0, :], bc(dram["pre_mix_w"])).then_inc(*tick("gain0", "mix", 16))
            weights(0)
            load_x(1)
            for u in range(1, RING):
                weights(u)
            sp.dma_start(gain[:, 1, :], bc(dram["post_mix_w"])).then_inc(*tick("gain1", "out", 16))
            for n, name in enumerate(("lambda_q1", "lambda_k1", "lambda_q2", "lambda_k2")):
                load_small(lam_in[:, n, :], bc(dram[name]), name)
            load_small(sub_w[:, :], bc(dram["subln_w"]), "subln_w")
            for t in range(TOKS):
                load_small(pos_i[:, t:t + 1], dram["positions_2"][:, t * P:(t + 1) * P].rearrange("a p -> p a"),
                           "positions")
            flat = gates1.rearrange("p g t d -> p (g t d)")
            for r in range(2):
                for h in range(NA_HEADS):
                    src = bass.AP(tensor=dram["rpb"].tensor,
                                  offset=h * RPB_HEAD + (5 - r) * RPB_ROW + NA_COLS - 1 - (GRID - 1),
                                  ap=[[1, GRID], [RPB_ROW, 6], [1, GRID]])
                    dst = flat[r * GRID:(r + 1) * GRID, h * 6 * GRID:(h + 1) * 6 * GRID]
                    sp.dma_start(dst.rearrange("p (t j) -> p t j", t=6), src)\
                        .then_inc(*tick("bias_loaded", (r, h), 16))
            for u in range(RING, n_units):
                weights(u)
                if u == FIRST["gate_b"] + 4:
                    sp.wait_ge(*at("scored", ("da", 7)))
                    for t in range(TOKS):
                        sp.dma_start(x[:, t, :], dram["x"][0, t * P:(t + 1) * P, :])\
                            .then_inc(*tick("x_again", None, 16))
                if u == FIRST["up0"] + 4 and last != 1:
                    sp.wait_ge(*at("merged", ("merged", 1)))
                    for key, dst, src in (("cq", cq_w, bc(dram["mla_norm_cq_2"])),
                                          ("ckv", ckv_w, bc(dram["mla_norm_ckv_2"])),
                                          ("gln", gln_w, bc(dram["gla_norm_2"])),
                                          ("gb", gb_w, bc(dram["gla_b_gate_2"])),
                                          ("gate2", wg2, dram["gla_w_gate2_2"][0])):
                        sp.dma_start(dst[:, :], src).then_inc(*tick("small2_loaded", None, 16))
                if u == 20:
                    sp.wait_ge(*at("pool", "bias_masked"))
                    for g in range(2):
                        for t in range(TOKS):
                            sp.dma_start(gates1[:, g, t, :], bc(dram["b_gate"][:, g * D:(g + 1) * D]))\
                                .then_inc(*tick("gate_bias", None, 16))
            for t in range(TOKS):
                if last == 1:
                    sp.wait_ge(*at("residual", ("down", t)))
                    src = x[:, t, :]
                else:
                    sp.wait_ge(*at("normed", ("final", t)))
                    src = row[:, t, :]
                sp.dma_start(out[0, t * P:(t + 1) * P, :], src).then_inc(*tick("stored", t, 16))
            sp.wait_ge(*at("stored", TOKS - 1))

        @block.scalar
        def _(act):
            split = [0]

            def advance(n):
                while split[0] < min(n, n_units):
                    u = split[0]
                    w = unit_width(UNITS[u][0])
                    act.wait_ge(*at(f"raw_loaded{u % RING}", u))
                    nc.scalar.activation(hi[:, u % RING, 0:w], raw[:, u % RING, 0:w], ACT.Copy)\
                        .then_inc(*tick("high_ready", u))
                    split[0] += 1

            def turned_high(key, bank, n, dst, kt0, t, scale=1.0):
                act.wait_ge(*at("turned", key))
                nc.scalar.activation(dst[0][:, kt0:kt0 + n, t * P:(t + 1) * P],
                                     aux[bank][:, 0:n * P].rearrange("p (k s) -> p k s", k=n), ACT.Copy,
                                     scale=scale).then_inc(*tick("turned_high", key))

            def sum_squares(src, junk, key):
                nc.scalar.activation(junk, src, ACT.Square, accum_out=stat(("ss", key))).then_inc(
                    *tick("sumsq", key))

            def pre_norm(tag, t):
                sum_squares(x[:, t, :], row[:, t, :], (tag, t))

            def take(name, t):
                a0, a1 = acc[:, 2 * t, :], acc[:, 2 * t + 1, :]
                if name not in ("branch_a", "branch_b", "gla_o", "mla_o", "out2", "down2"):
                    act.wait_ge(*at("mm_done", (name, t)))
                if name == "qk_a":
                    nc.scalar.activation(row[:, t, :].rearrange("p (b c) -> p b c", b=2), acc_of(t), ACT.Copy)\
                        .then_inc(*tick("acc_act", (name, t)))
                elif name in ("v_a_q_b", "k_b_v_b"):
                    act.wait_ge(*at("turned", ("qk_a", t, 1) if name == "v_a_q_b" else ("q_b", t)))
                    nc.scalar.activation(row[:, t, 0:512], a1 if name == "v_a_q_b" else a0, ACT.Copy)\
                        .then_inc(*tick("acc_act", (name, t)))
                elif name in ("gate_a", "gate_b"):
                    g = gates1[:, int(name == "gate_b"), t, :]
                    act.wait_ge(*at("vec", ("gate_sum", name, t)))
                    nc.scalar.activation(g, g, ACT.Tanh, scale=0.5).then_inc(*tick("act", ("gate", name, t)))
                elif name in ("gate_a2", "gate_b2"):
                    g = (ga2 if name == "gate_a2" else gb2)[:, t, :]
                    nc.scalar.activation(g.rearrange("p (b c) -> p b c", b=2), acc_of(t), ACT.Tanh, scale=0.5)\
                        .then_inc(*tick("acc_act", (name, t)))
                elif name in ("out", "down"):
                    sum_squares(acc_of(t), row[:, t, :].rearrange("p (b c) -> p b c", b=2), ("post_" + name, t))
                elif name.startswith("up"):
                    w = SC[name][3][0][2]
                    if name[-1] != "0":
                        act.wait_ge(*at("turned", (name[:-1] + str(int(name[-1]) - 1), t)))
                    nc.scalar.activation(fe[:, t, 0:w], a0[:, 0:w], ACT.Tanh, scale=0.5)\
                        .then_inc(*tick("act", ("ffn_tanh", name, t)))
                elif name == "latent":
                    sum_squares(a0[:, 0:Q_RANK], row[:, t, 0:Q_RANK], ("cq", t))
                    sum_squares(a1[:, 0:KV_RANK], row[:, t, Q_RANK:Q_RANK + KV_RANK], ("ckv", t))
                elif name == "gla_qkv":
                    nc.scalar.activation(gqk[:, t, :], a0, ACT.Copy).then_inc(*tick("acc_act", (name, t)))
                elif name == "gla_og":
                    nc.scalar.activation(lr[:, t, :], a1[:, 0:16], ACT.Copy).then_inc(*tick("act", ("lr", t)))
                    nc.scalar.activation(sil[:, t, :], a0, ACT.Tanh, scale=0.5)\
                        .then_inc(*tick("act", ("og_tanh", t)))
                elif name == "uq":
                    act.wait_ge(*at("turned", ("latent", t, 1)))
                    nc.scalar.activation(row[:, t, 0:768].rearrange("p (b c) -> p b c", b=2),
                                         acc_of(t)[:, :, 0:384], ACT.Copy, scale=-1.0)\
                        .then_inc(*tick("acc_act", (name, t)))
                elif name == "ukv":
                    nc.scalar.activation(
                        ktm[:, t, :, 0:NOPE].rearrange("p (b h) d -> p b h d", b=2),
                        acc_of(t).rearrange("p b (h d) -> p b h d", d=P)[:, :, :, 0:NOPE], ACT.Copy)\
                        .then_inc(*tick("acc_act", (name, t)))
                nxt = {"out": "ffn", "down": "mix2", "out2": "ffn2", "down2": "final"}.get(name)
                if nxt and not (last == 1 and name == "down"):
                    act.wait_ge(*at("residual", (name, t)))
                    pre_norm(nxt, t)

            GAIN0 = {"mix": ("ffn", "pre_ffn_w"), "ffn": ("mix2", "ln_mix_2"), "mix2": ("ffn2", "ln_ffn_2")}
            GAIN1 = {"ffn": ("down", "post_ffn_w"), "mix2": ("final", "final_norm_2")}

            def step(kind, *a):
                if kind == "first_norm":
                    act.wait_ge(*at(f"x_loaded{a[0]}"))
                    pre_norm("mix", a[0])
                elif kind == "setup":
                    act.wait_ge(*at("vec", "sin_args"))
                    nc.scalar.activation(sin[:, :, :], sin[:, :, :], ACT.Sin)
                    for n in range(2):
                        i = nc.scalar.activation(cos2[:, :, n, :], angle[:, :, :], ACT.Sin)
                    i.then_inc(*tick("act", "rotary"))
                    act.wait_ge(*at("vec", "lambda_dots"))
                    nc.scalar.activation(lam[:, 0:2], lam[:, 0:2], ACT.Exp).then_inc(*tick("act", "lambda_exp"))
                elif kind == "norm_turn":
                    tag, t = a
                    for b in range(2):
                        turned_high((tag, t, b), 2 * t + b, 4, hT, 4 * b, t,
                                    0.5 if tag.startswith("merged") else 1.0)
                    if t == TOKS - 1:
                        for n, table in enumerate((GAIN0, GAIN1)):
                            if tag in table:
                                key, src = table[tag]
                                src = ins[src]
                                src = src if len(src.shape) == 2 else src.rearrange("(a n) -> a n", a=1)
                                act.dma_start(gain[:, n, :], src.to_broadcast([P, D]))\
                                    .then_inc(*tick(f"gain{n}", key, 16))
                elif kind == "qk_a_turn":
                    t, = a
                    act.wait_ge(*at("turned", ("qk_a", t, 1)))
                    nc.scalar.activation(kaT[:, :, t * P:(t + 1) * P],
                                         aux[2 * t + 1][:, :].rearrange("p (k s) -> p k s", k=4), ACT.Copy)\
                        .then_inc(*tick("turned_out", ("k_a", t)))
                elif kind == "q_b_turn":
                    t, = a
                    act.wait_ge(*at("turned", ("q_b", t)))
                    for hb in range(2):
                        s = slice(hb * HD, hb * HD + HD)
                        i = nc.scalar.activation(qbT[s, hb, :, t * P:(t + 1) * P],
                                                 aux[2][s, :].rearrange("p (k s) -> p k s", k=4),
                                                 ACT.Copy, scale=-HD ** -0.5)
                    i.then_inc(*tick("turned_out", ("q_b", t)))
                elif kind == "k_b_turn":
                    t, = a
                    act.wait_ge(*at("turned", ("k_b", t)))
                    nc.scalar.activation(kbT[:, :, t * P:(t + 1) * P],
                                         aux[2][:, :].rearrange("p (k s) -> p k s", k=4), ACT.Copy)\
                        .then_inc(*tick("turned_out", ("k_b", t)))
                elif kind == "score":
                    kind, i = a
                    n = att_keys(kind, i)
                    T = probs[kind]
                    act.wait_ge(*at("logits", (kind, i)))
                    for hb in range(2):
                        j = nc.scalar.activation(T[:, i % 2, hb * 256:hb * 256 + n], T[:, i % 2, hb * 256:hb * 256 + n],
                                                 ACT.Exp, scale=-1.0, bias=stat(("min", kind, i), 2)[:, hb:hb + 1],
                                                 accum_out=stat(("sum", kind, i // 4), 8)[
                                                     :, 2 * (i % 4) + hb:2 * (i % 4) + hb + 1])
                        j.then_inc(*tick("probs", (kind, i)))
                elif kind == "turn_p":
                    kind, i = a
                    act.wait_ge(*at("turned", ("p", kind, i)))
                    if i >= 2:
                        act.wait_ge(*at("pv_done", (kind, i - 2)))
                    w = {"da": 1, "na": 2, "mla": 2}[kind]
                    n = att_keys(kind, i)
                    nc.scalar.activation(
                        probs_T[kind][:, i % 2, 0:w * 256].rearrange("p (h n) -> p h n", h=w)[:, :, 0:n],
                        aux[2][:, 0:w * 256].rearrange("p (h n) -> p h n", h=w)[:, :, 0:n], ACT.Copy)\
                        .then_inc(*tick("turned_out", ("p", kind, i)))
                elif kind == "da_norm":
                    qt, = a
                    act.wait_ge(*at("pv_done", ("da", 4 * qt + 3)))
                    nc.scalar.activation(row[:, qt, 512:1024], aux[3][:, :], ACT.Copy)\
                        .then_inc(*tick("act", ("da_rows", qt)))
                    if qt:
                        act.wait_ge(*at("turned", ("y", "da", qt - 1)))
                    nc.scalar.activation(ob1[:, :], aux[3][:, :], ACT.Square).then_inc(*tick("act", ("da_sq", qt)))
                elif kind == "turn_y":
                    kind, t = a
                    turned_high(("y", kind, t), 2, 4, yT, {"da": 0, "na": 4, "mla": 0, "gla": 4}[kind], t)
                elif kind == "ffn_turn":
                    name, t = a
                    j = int(name[-1])
                    n = SC[name][3][0][2] // P
                    f = (yT, 4 * j) if j < 2 else (fT, 4 * j - KD)
                    turned_high((name, t), (2 * j + t) % 4, n, f[0], f[1], t)
                elif kind == "latent_turn":
                    t, = a
                    turned_high(("latent", t, 0), 2 * t, 4, yT, 0, t)
                    turned_high(("latent", t, 1), 2 * t + 1, 1, yT, 4, t)
                elif kind == "gla_qk_turn":
                    t, = a
                    act.wait_ge(*at("turned", ("gla_qk", t)))
                    for T, c, s in ((gqT, 0, GLA_DK ** -0.5), (gkT, 256, 1.0)):
                        i = nc.scalar.activation(T[:, :, t * P:(t + 1) * P],
                                                 aux[2 + t][:, c:c + 256].rearrange("p (k s) -> p k s", k=2),
                                                 ACT.Copy, scale=s)
                    i.then_inc(*tick("turned_out", ("gla_qk", t)))
                elif kind == "gate_lr_turn":
                    t, = a
                    act.wait_ge(*at("turned", ("lr", t)))
                    nc.scalar.activation(lrT[:, t * P:(t + 1) * P], aux[2 + t][0:16, 0:P], ACT.Copy)\
                        .then_inc(*tick("turned_out", ("lr", t)))
                elif kind == "decay_logits":
                    act.wait_ge(*at("vec", "abs_z"))
                    nc.scalar.activation(gz[:, :, :], gz[:, :, :], ACT.Exp, scale=-1.0)\
                        .then_inc(*tick("act", "exp_abs_z"))
                    act.wait_ge(*at("act", "exp_abs_z"))
                    act.wait_ge(*at("pool", "one_plus"))
                    nc.scalar.activation(gz[:, :, :], gz[:, :, :], ACT.Ln).then_inc(*tick("act", "ln"))
                elif kind == "decay_sums":
                    act.wait_ge(*at("gla_done", "sums"))
                    nc.scalar.activation(bT[:, :, :], aux[0][:, :].rearrange("p (f s) -> p f s", f=2), ACT.Copy)\
                        .then_inc(*tick("act", "bT"))
                    nc.scalar.activation(kdec[:, :, :], aux[1][:, :].rearrange("p (t f) -> p t f", t=2), ACT.Exp)\
                        .then_inc(*tick("act", "kdec_exp"))
                    act.wait_ge(*at("act", "bT"))
                    for hb in range(2):
                        s = slice(hb * 64, hb * 64 + 64)
                        nc.scalar.activation(qdec[s, hb, :, :], bT[s, :, :], ACT.Exp)\
                            .then_inc(*tick("act", "qdec_exp"))
                    nc.scalar.activation(
                        dchunk[:, :, :], bT.rearrange("p f (c s) -> p f c s", c=4)[:, :, :, GLA_CHUNK - 1], ACT.Exp)\
                        .then_inc(*tick("act", "dchunk"))
                elif kind == "gla_decay":
                    n, = a
                    act.wait_ge(*at("vec", ("level_diff", n)))
                    nc.scalar.activation(ED[:, :], ED[:, :], ACT.Exp).then_inc(*tick("act", ("level_exp", n)))
                elif kind == "gla_output":
                    t, = a
                    act.wait_ge(*at("gla_done", ("out", t)))
                    nc.scalar.activation(ob2[:, t, :], aux[t][:, :], ACT.Square).then_inc(*tick("act", ("gla_sq", t)))
                elif kind == "mla_turn":
                    t, = a
                    for b in range(4):
                        act.wait_ge(*at("turned", ("mla", t, b)))
                        dst = (qmT, kmT)[b // 2]
                        nc.scalar.activation(dst[:, 4 * (b % 2):4 * (b % 2) + 4, t * P:(t + 1) * P],
                                             aux[b][0:MLA_QK, :].rearrange("p (k s) -> p k s", k=4), ACT.Copy)\
                            .then_inc(*tick("turned_out", ("mla", t, b)))

            for i, st in enumerate(steps):
                if st[0] == "mm":
                    advance(ahead_of(i))
                elif st[0] == "take":
                    take(*st[1:])
                elif st[0] == "ahead":
                    advance(st[1])
                else:
                    step(*st[1:])

        @block.tensor
        def _(pe):
            reader = {}
            acc_reader = {}

            def operand_key(tag, t):
                if tag.startswith("y_"):
                    return ("y", tag[2:], t)
                return (tag, t, 1)

            def into(bank):
                if bank in reader:
                    pe.wait_ge(*at(*reader[bank]))

            def turn(key, bank, tiles, read):
                into(bank)
                for n, src in enumerate(tiles):
                    w = src.shape[-1]
                    i = nc.tensor.transpose(aux[bank][0:w, n * P:(n + 1) * P], src, ident[:, :])
                i.then_inc(*tick("turned", key))
                reader[bank] = read

            def slices(ap, n):
                return [ap[:, k * P:(k + 1) * P] for k in range(n)]

            ACC_READ = {"qk_a": ("acc_act",), "v_a_q_b": ("acc_act", "acc_vec"), "k_b_v_b": ("acc_act", "acc_vec"),
                        "gate_a2": ("acc_act",), "gate_b2": ("acc_act",), "gla_qkv": ("acc_act", "acc_vec"),
                        "uq": ("acc_act",), "ukv": ("acc_act", "acc_vec"), "out2": ("residual",), "down2": ("residual",)}

            def product(name, t, kt):
                u = FIRST[name] + kt
                pieces = SC[name][3]
                kts = SC[name][2]
                if kt == 0:
                    for s in acc_reader.get(t, ()):
                        pe.wait_ge(*at(*s))
                    if name in OPERAND_READY:
                        pe.wait_ge(*at("turned_low", operand_key(OPERAND_READY[name], t)))
                if name in ("down", "down2") and kt % 4 == 0:
                    pe.wait_ge(*at("turned_low", (name.replace("down", "up") + str(kt // 4), t)))
                if t == 0:
                    pe.wait_ge(*at("low_ready", u))
                (xh, xl), k0 = operand(name, kt)
                sl = slice(t * P, (t + 1) * P)
                for n, (lhs, w) in enumerate(((xh, hi), (xh, lo), (xl, hi))):
                    for b, (_, _, width, d) in enumerate(pieces):
                        i = nc.tensor.matmul(acc[:, 2 * t + b, 0:width], lhs[:, k0, sl],
                                             w[:, u % RING, d:d + width],
                                             start=(kt == 0 and n == 0), stop=(kt == kts - 1 and n == 2))
                if kt == kts - 1:
                    i.then_inc(*tick("mm_done", (name, t)))
                    if name in ("gate_a", "gate_b"):
                        acc_reader[t] = [("vec", ("gate_sum", name, t))]
                    else:
                        acc_reader[t] = [(s, (name, t)) for s in ACC_READ.get(name, ("acc_vec",))]
                elif t == TOKS - 1:
                    i.then_inc(*tick("weights_used", u))

            def step(kind, *a):
                if kind == "norm_turn":
                    tag, t = a
                    src = ("merged", (tag, t)) if tag.startswith("merged") else ("normed", (tag, t))
                    pe.wait_ge(*at(*src))
                    for b in range(2):
                        turn((tag, t, b), 2 * t + b, slices(row[:, t, 512 * b:512 * b + 512], 4),
                             ("turned_low", (tag, t, b)))
                elif kind == "qk_a_turn":
                    t, = a
                    pe.wait_ge(*at("acc_act", ("qk_a", t)))
                    for b, r in ((0, ("vec", ("q_a", t))), (1, ("turned_out", ("k_a", t)))):
                        turn(("qk_a", t, b), 2 * t + b, slices(row[:, t, 512 * b:512 * b + 512], 4), r)
                elif kind in ("q_b_turn", "k_b_turn"):
                    t, = a
                    pe.wait_ge(*at("acc_act", ("v_a_q_b" if kind == "q_b_turn" else "k_b_v_b", t)))
                    turn((kind[:3], t), 2, slices(row[:, t, 0:512], 4), ("turned_out", (kind[:3], t)))
                elif kind == "score":
                    kind, i = a
                    if i % 4 == 0:
                        if kind == "da":
                            pe.wait_ge(*at("vec", ("q_a", 1)))
                            pe.wait_ge(*at("turned_out", ("k_a", 1)))
                            pe.wait_ge(*at("pool", "q_zero"))
                        elif kind == "na":
                            pe.wait_ge(*at("turned_out", ("k_b", 1)))
                        else:
                            pe.wait_ge(*at("turned_out", ("mla", 1, 3)))
                    into(i % 2)
                    n = att_keys(kind, i)
                    for hb in range(2):
                        m = nc.tensor.matmul(aux[i % 2][:, hb * 256:hb * 256 + n], att_q(kind, hb, i),
                                             att_k(kind, hb, i), start=True, stop=True)
                    m.then_inc(*tick("scored", (kind, i)))
                    reader[i % 2] = ("logits", (kind, i))
                elif kind == "turn_p":
                    kind, i = a
                    T = probs[kind]
                    pe.wait_ge(*at(*((("vec", ("combined", i)) if kind == "da" else ("probs", (kind, i))))))
                    into(2)
                    for hb in range(1 if kind == "da" else 2):
                        for kt in range(att_keys(kind, i) // P):
                            m = nc.tensor.transpose(aux[2][:, hb * 256 + kt * P:hb * 256 + (kt + 1) * P],
                                                    T[:, i % 2, hb * 256 + kt * P:hb * 256 + (kt + 1) * P],
                                                    ident[:, :])
                    m.then_inc(*tick("turned", ("p", kind, i)))
                    reader[2] = ("turned_out", ("p", kind, i))
                elif kind == "pv":
                    kind, i = a
                    qt, n = divmod(i, 4)
                    pe.wait_ge(*at("turned_out", ("p", kind, i)))
                    if i == 0:
                        v, s = {"da": (va, ("acc_vec", ("v_a_q_b", 1))), "na": (vb, ("acc_vec", ("k_b_v_b", 1))),
                                "mla": (vm, ("acc_vec", ("ukv", 1)))}[kind]
                        pe.wait_ge(*at(*s))
                    v = {"da": va, "na": vb, "mla": vm}[kind]
                    if n == 0:
                        into(3)
                    kts = att_keys(kind, i) // P
                    for hb in range(1 if kind == "da" else 2):
                        c = slice(n * P, n * P + P) if kind == "da" else \
                            slice((2 * n + hb) * HD, (2 * n + hb) * HD + HD)
                        for kt in range(kts):
                            m = nc.tensor.matmul(aux[3][:, c],
                                                 probs_T[kind][:, i % 2, hb * 256 + kt * P:hb * 256 + (kt + 1) * P],
                                                 v[:, kt, c], start=(kt == 0), stop=(kt == kts - 1))
                    m.then_inc(*tick("pv_done", (kind, i)))
                    reader[3] = ("act", ("da_sq", qt)) if kind == "da" else ("vec", ("heads", kind, qt))
                elif kind == "turn_y":
                    kind, t = a
                    src = ob2[:, t, :] if kind == "gla" else (ob2[:, t, :] if kind == "mla" else ob1[:, :])
                    pe.wait_ge(*at(*(("pool", ("y", kind, t)) if kind == "gla" else ("vec", ("y", kind, t)))))
                    turn(("y", kind, t), 2, slices(src, 4), ("turned_low", ("y", kind, t)))
                elif kind == "ffn_turn":
                    name, t = a
                    pe.wait_ge(*at("acc_vec", (name, t)))
                    j = int(name[-1])
                    turn((name, t), (2 * j + t) % 4, slices(fe[:, t, :], SC[name][3][0][2] // P),
                         ("turned_low", (name, t)))
                elif kind == "latent_turn":
                    t, = a
                    pe.wait_ge(*at("vec", ("latent", t)))
                    turn(("latent", t, 0), 2 * t, slices(row[:, t, 0:512], 4), ("turned_low", ("latent", t, 0)))
                    turn(("latent", t, 1), 2 * t + 1, slices(row[:, t, 512:640], 1), ("turned_low", ("latent", t, 1)))
                elif kind == "gla_qk_turn":
                    t, = a
                    pe.wait_ge(*at("acc_act", ("gla_qkv", t)))
                    turn(("gla_qk", t), 2 + t, slices(gqk[:, t, :], 4), ("turned_out", ("gla_qk", t)))
                elif kind == "gate_lr_turn":
                    t, = a
                    pe.wait_ge(*at("act", ("lr", t)))
                    turn(("lr", t), 2 + t, [lr[:, t, :]], ("turned_out", ("lr", t)))
                elif kind == "decay_logits":
                    into(0)
                    pe.wait_ge(*at("small2_loaded"))
                    pe.wait_ge(*at("turned_out", ("lr", 1)))
                    for t in range(TOKS):
                        m = nc.tensor.matmul(aux[0][:, t * 256:t * 256 + 256], lrT[:, t * P:(t + 1) * P], wg2[:, :],
                                             start=True, stop=True)
                    m.then_inc(*tick("gla_done", "logits"))
                    reader[0] = ("vec", "z")
                elif kind == "decay_sums":
                    pe.wait_ge(*at("vec", "log_decay"))
                    pe.wait_ge(*at("pool", "sum_masks"))
                    into(0)
                    into(1)
                    for f in range(2):
                        for t in range(TOKS):
                            c = (2 * f + t) * P
                            nc.tensor.matmul(aux[0][:, c:c + P], gl[:, t, f * P:(f + 1) * P], upto[:, :],
                                             start=True, stop=True)
                    for t in range(TOKS):
                        m = nc.tensor.matmul(aux[1][:, t * 256:t * 256 + 256], after[:, :], gl[:, t, :],
                                             start=True, stop=True)
                    m.then_inc(*tick("gla_done", "sums"))
                    reader[0] = ("act", "bT")
                    reader[1] = ("act", "kdec_exp")
                elif kind == "gla_level":
                    n, = a
                    if n == 0:
                        pe.wait_ge(*at("turned_out", ("gla_qk", 1)))
                        q, k = gqT, gkT
                    else:
                        pe.wait_ge(*at("pool", ("level_q", n - 1)))
                        pe.wait_ge(*at("vec", ("level_k", n - 1)))
                        q, k = QE, KE
                    for hb in range(2):
                        b = 2 * (n % 2) + hb
                        into(b)
                        r = slice(hb * 64, hb * 64 + 64)
                        for t in range(TOKS):
                            for f in range(2):
                                for c in range(2):
                                    s = slice(t * P + c * 64, t * P + c * 64 + 64)
                                    m = nc.tensor.matmul(
                                        aux[b][c * 64:c * 64 + 64, (2 * t + f) * 64:(2 * t + f) * 64 + 64],
                                        k[r, f, s], q[r, f, s], start=True, stop=True)
                        reader[b] = ("vec", ("level", n))
                    m.then_inc(*tick("gla_done", ("level", n)))
                elif kind == "gla_state":
                    pe.wait_ge(*at("pool", "kdec"))
                    into(2)
                    into(3)
                    pe.wait_ge(*at("acc_vec", ("gla_qkv", 1)))
                    for c, b, col in ((0, 2, 0), (2, 2, 256), (1, 3, 0)):
                        r = slice((c % 2) * 64, (c % 2) * 64 + 64)
                        for h in range(GLA_H):
                            f, hb = divmod(h, 2)
                            m = nc.tensor.matmul(aux[b][hb * 64:hb * 64 + 64, col + f * P:col + f * P + P],
                                                 kdec[r, c // 2, h * 64:h * 64 + 64],
                                                 gv[r, c // 2, h * P:h * P + P], start=True, stop=True)
                    m.then_inc(*tick("gla_done", "state"))
                    reader[2] = reader[3] = ("vec", "states")
                elif kind == "gla_output":
                    t, = a
                    pe.wait_ge(*at("vec", "states"))
                    pe.wait_ge(*at("pool", "qdec"))
                    pe.wait_ge(*at("pool", "attn_blocks"))
                    into(t)
                    for h in range(GLA_H):
                        f, hb = divmod(h, 2)
                        o = slice(h * P, h * P + P)
                        nc.tensor.matmul(aux[t][:, o], AT[:, t, f, hb, :, :].rearrange("p c i -> p (c i)"),
                                         gv[:, t, o], start=True, stop=(False if t else False), skip_group_check=True)
                        for c in range(2):
                            ch = 2 * t + c
                            if ch:
                                m = nc.tensor.matmul(aux[t][c * 64:c * 64 + 64, o],
                                                     qdec[:, hb, f, ch * 64:ch * 64 + 64], ST[:, ch - 1, f, :],
                                                     start=False, stop=True, skip_group_check=True)
                    m.then_inc(*tick("gla_done", ("out", t)))
                    reader[t] = ("vec", ("gla_heads", t))
                elif kind == "mla_turn":
                    t, = a
                    pe.wait_ge(*at("vec", ("q_rotated", t)))
                    pe.wait_ge(*at("vec", ("k_rotated", t)))
                    pe.wait_ge(*at("acc_act", ("ukv", t)))
                    for b in range(4):
                        src = (row[:, t, 0:768].rearrange("p (h d) -> p h d", h=MLA_H), ktm[:, t, :, :])[b // 2]
                        turn(("mla", t, b), b, [src[:, 4 * (b % 2) + n, :] for n in range(4)],
                             ("turned_out", ("mla", t, b)))

            pe.wait_ge(*at("pool", "ident"))
            for n in range(32):
                nc.tensor.transpose(aux[3][:, 0:P], ident[:, :], ident[:, :])
            for st in steps:
                if st[0] not in ("take", "ahead"):
                    (product if st[0] == "mm" else step)(*st[1:])

        @block.vector
        def _(dve):
            split = [0]

            def advance(n):
                while split[0] < min(n, n_units):
                    u = split[0]
                    w = unit_width(UNITS[u][0])
                    dve.wait_ge(*at("high_ready", u))
                    nc.vector.tensor_tensor(lo[:, u % RING, 0:w], raw[:, u % RING, 0:w],
                                            hi[:, u % RING, 0:w].bitcast(F32), ALU.subtract)\
                        .then_inc(*tick("low_ready", u))
                    split[0] += 1

            def then(i):
                i.then_inc(*tick("vec_chain"))
                dve.wait_ge(*last_of("vec_chain"))

            def signal(i, name, key, wait=False):
                i.then_inc(*tick(name, key))
                if wait:
                    dve.wait_ge(*last_of(name))

            def turned_low(key, bank, n, dst, kt0, t, scale=1.0):
                dve.wait_ge(*at("turned_high", key))
                s = slice(t * P, (t + 1) * P)
                nc.vector.scalar_tensor_tensor(dst[1][:, kt0:kt0 + n, s],
                                               aux[bank][:, 0:n * P].rearrange("p (k s) -> p k s", k=n), scale,
                                               dst[0][:, kt0:kt0 + n, s].bitcast(F32), ALU.mult, ALU.subtract)\
                    .then_inc(*tick("turned_low", key))

            def normed(tag, t, g):
                dve.wait_ge(*at("rstd", (tag, t)))
                dve.wait_ge(*at(f"gain{g}", tag))
                nc.vector.scalar_tensor_tensor(row[:, t, :], x[:, t, :], stat(("rstd", (tag, t))), gain[:, g, :],
                                               ALU.mult, ALU.mult).then_inc(*tick("normed", (tag, t)))

            def bcast(ap, n):
                return ap.rearrange("p (k o) -> p k o", o=1).to_broadcast([P, ap.shape[1], n])

            def take(name, t):
                a0, a1 = acc[:, 2 * t, :], acc[:, 2 * t + 1, :]
                dve.wait_ge(*at("mm_done", (name, t)))
                two = lambda ap: ap.rearrange("p (b c) -> p b c", b=2)
                if name == "v_a_q_b":
                    signal(nc.vector.tensor_copy(va[:, t, :], a0), "acc_vec", (name, t))
                elif name == "k_b_v_b":
                    signal(nc.vector.tensor_copy(vb[:, t, :], a1), "acc_vec", (name, t))
                elif name == "gla_qkv":
                    signal(nc.vector.tensor_copy(gv[:, t, :], a1), "acc_vec", (name, t))
                elif name in ("gate_a", "gate_b"):
                    g = gates1[:, int(name == "gate_b"), t, :]
                    dve.wait_ge(*at("gate_bias"))
                    i = nc.vector.tensor_tensor(two(g), acc_of(t), two(g), ALU.add)
                    i.then_inc(*tick("vec", ("gate_sum", name, t)))
                elif name in ("branch_a", "gla_o"):
                    g = gates1[:, 0, t, :] if name == "branch_a" else gb2[:, t, :]
                    dve.wait_ge(*at(*(("act", ("gate", "gate_a", t)) if name == "branch_a" else
                                      ("acc_act", ("gate_b2", t)))))
                    signal(nc.vector.scalar_tensor_tensor(two(row[:, t, :]), two(g), 1.0, acc_of(t), ALU.add,
                                                          ALU.mult), "acc_vec", (name, t))
                elif name in ("branch_b", "mla_o"):
                    g = gates1[:, 1, t, :] if name == "branch_b" else ga2[:, t, :]
                    dve.wait_ge(*at(*(("act", ("gate", "gate_b", t)) if name == "branch_b" else
                                      ("acc_act", ("gate_a2", t)))))
                    signal(nc.vector.scalar_tensor_tensor(two(g), two(g), 1.0, acc_of(t), ALU.add, ALU.mult),
                           "acc_vec", (name, t), True)
                    signal(nc.vector.tensor_tensor(row[:, t, :], row[:, t, :], g, ALU.add),
                           "merged", ("merged" if name == "branch_b" else "merged2", t))
                elif name in ("out", "down"):
                    dve.wait_ge(*at("rstd", ("post_" + name, t)))
                    dve.wait_ge(*at("gain1", name))
                    signal(nc.vector.scalar_tensor_tensor(two(row[:, t, :]), acc_of(t),
                                                          stat(("rstd", ("post_" + name, t))), two(gain[:, 1, :]),
                                                          ALU.mult, ALU.mult), "acc_vec", (name, t), True)
                    if name == "out":
                        dve.wait_ge(*at("x_again"))
                    signal(nc.vector.tensor_tensor(x[:, t, :], x[:, t, :], row[:, t, :], ALU.add),
                           "residual", (name, t))
                elif name in ("out2", "down2"):
                    i = nc.vector.tensor_tensor(two(x[:, t, :]), acc_of(t), two(x[:, t, :]), ALU.add)
                    i.then_inc(*tick("residual", (name, t)))
                elif name.startswith("up"):
                    w = SC[name][3][0][2]
                    e = fe[:, t, 0:w]
                    dve.wait_ge(*at("act", ("ffn_tanh", name, t)))
                    then(nc.vector.scalar_tensor_tensor(e, e, 1.0, a0[:, 0:w], ALU.add, ALU.mult))
                    signal(nc.vector.scalar_tensor_tensor(e, e, 0.5, a1[:, 0:w], ALU.mult, ALU.mult),
                           "acc_vec", (name, t))
                elif name == "latent":
                    dve.wait_ge(*at("small2_loaded"))
                    for key, g, s, src in (("cq", cq_w, slice(0, Q_RANK), a0[:, 0:Q_RANK]),
                                           ("ckv", ckv_w, slice(Q_RANK, Q_RANK + KV_RANK), a1[:, 0:KV_RANK])):
                        dve.wait_ge(*at("rstd", (key, t)))
                        i = nc.vector.scalar_tensor_tensor(row[:, t, s], src, stat(("rstd", (key, t))), g[:, :],
                                                           ALU.mult, ALU.mult)
                    signal(i, "vec", ("latent", t))
                    signal(nc.vector.tensor_copy(kr[:, t, :, :].rearrange("p a b -> p (a b)"),
                                                 a1[:, KV_RANK:KV_RANK + ROPE]), "acc_vec", (name, t), True)
                    r = rt[:, 0, 0:2, :, :]
                    then(nc.vector.tensor_tensor(r[:, 0, :, :], kr[:, t, :, :], cos2[:, t, :, :], ALU.mult))
                    then(nc.vector.tensor_tensor(r[:, 1, 0, :], kr[:, t, 1, :], sin[:, t, :], ALU.mult))
                    then(nc.vector.tensor_tensor(r[:, 1, 1, :], kr[:, t, 0, :], sin[:, t, :], ALU.mult))
                    then(nc.vector.tensor_tensor(kr[:, t, 0, :], r[:, 0, 0, :], r[:, 1, 0, :], ALU.subtract))
                    then(nc.vector.tensor_tensor(kr[:, t, 1, :], r[:, 0, 1, :], r[:, 1, 1, :], ALU.add))
                elif name == "gla_og":
                    s = sil[:, t, :]
                    dve.wait_ge(*at("act", ("og_tanh", t)))
                    signal(nc.vector.scalar_tensor_tensor(s, s, 1.0, a0, ALU.add, ALU.mult), "acc_vec", (name, t))
                    if t == 0:
                        signal(nc.vector.tensor_scalar(gln_w[:, :], gln_w[:, :], 0.5, None, ALU.mult), "vec", "gln")
                elif name == "uq":
                    dve.wait_ge(*at("acc_act", (name, t)))
                    q = row[:, t, 0:768].rearrange("p (h d) -> p h d", h=MLA_H)[:, :, NOPE:MLA_QK]
                    c = cos2[:, t, :, :].rearrange("p a b -> p (a b)").rearrange("p (o d) -> p o d", o=1)\
                        .to_broadcast([P, MLA_H, ROPE])
                    s = sin[:, t, :].rearrange("p (o d) -> p o d", o=1).to_broadcast([P, MLA_H, 16])
                    A = rt[:, 0, :, :, :].rearrange("p h a d -> p h (a d)")
                    B = rt[:, 1, :, :, :].rearrange("p h a d -> p h (a d)")
                    then(nc.vector.tensor_tensor(A, q, c, ALU.mult))
                    then(nc.vector.tensor_tensor(B[:, :, 0:16], q[:, :, 16:32], s, ALU.mult))
                    then(nc.vector.tensor_tensor(B[:, :, 16:32], q[:, :, 0:16], s, ALU.mult))
                    then(nc.vector.tensor_tensor(q[:, :, 0:16], A[:, :, 0:16], B[:, :, 0:16], ALU.subtract))
                    signal(nc.vector.tensor_tensor(q[:, :, 16:32], A[:, :, 16:32], B[:, :, 16:32], ALU.add),
                           "vec", ("q_rotated", t), True)
                elif name == "ukv":
                    dve.wait_ge(*at("acc_act", (name, t)))
                    signal(nc.vector.tensor_copy(
                        vm[:, t, :].rearrange("p (b h d) -> p b h d", b=2, h=4),
                        acc_of(t).rearrange("p b (h d) -> p b h d", d=P)[:, :, :, NOPE:P]), "acc_vec", (name, t))
                    k = kr[:, t, :, :].rearrange("p a b -> p (a b)").rearrange("p (o d) -> p o d", o=1)\
                        .to_broadcast([P, MLA_H, ROPE])
                    signal(nc.vector.tensor_copy(ktm[:, t, :, NOPE:MLA_QK], k), "vec", ("k_rotated", t))
                nxt = {"out": "ffn", "down": "mix2", "out2": "ffn2", "down2": "final"}.get(name)
                if nxt and not (last == 1 and name == "down"):
                    normed(nxt, t, 1 if nxt == "final" else 0)

            def step(kind, *a):
                if kind == "first_norm":
                    normed("mix", a[0], 0)
                elif kind == "setup":
                    setup()
                elif kind == "norm_turn":
                    tag, t = a
                    for b in range(2):
                        turned_low((tag, t, b), 2 * t + b, 4, hT, 4 * b, t,
                                   0.5 if tag.startswith("merged") else 1.0)
                elif kind == "qk_a_turn":
                    t, = a
                    dve.wait_ge(*at("turned", ("qk_a", t, 0)))
                    for c in range(2):
                        s = slice(c * HD, c * HD + HD)
                        i = nc.vector.tensor_tensor(
                            qaT[s, c, :, t * P:(t + 1) * P], aux[2 * t][s, :].rearrange("p (k s) -> p k s", k=4),
                            stat("q_scale", 4)[s, :].rearrange("p (k o) -> p k o", o=1).to_broadcast([HD, 4, P]),
                            ALU.mult)
                    signal(i, "vec", ("q_a", t))
                elif kind == "score":
                    kind, i = a
                    qt, n = divmod(i, 4)
                    T = probs[kind]
                    keys = att_keys(kind, i)
                    dve.wait_ge(*at("scored", (kind, i)))
                    if kind == "na" and i == 0:
                        dve.wait_ge(*at("pool", "bias_masked"))
                    if kind == "mla" and i == 0:
                        dve.wait_ge(*at("pool", "causal"))
                    if i >= 2:
                        dve.wait_ge(*at("turned", ("p", kind, i - 2)))
                    elif kind == "na":
                        dve.wait_ge(*at("turned", ("p", "da", 6 + i)))
                    for hb in range(2):
                        if kind == "da":
                            add, scale = dist[:, qt, :], 4.0 ** -(n + 1)
                        elif kind == "na":
                            add, scale = nbias[:, 2 * n + hb, 2 - 2 * qt:6 - 2 * qt, :].rearrange(
                                "p t j -> p (t j)"), 1.0
                        else:
                            add, scale = causal[:, SEQ - keys:SEQ], MLA_QK ** -0.5
                        nc.vector.tensor_tensor_reduce(
                            out=T[:, i % 2, hb * 256:hb * 256 + keys], in0=aux[i % 2][:, hb * 256:hb * 256 + keys],
                            in1=add, scale=scale, scalar=BIG, op0=ALU.add, op1=ALU.min,
                            accum_out=stat(("min", kind, i), 2)[:, hb:hb + 1]).then_inc(*tick("logits", (kind, i)))
                elif kind == "combine":
                    i, = a
                    T = T1[:, i % 2, :]
                    dve.wait_ge(*at("probs", ("da", i)))
                    if i == 0:
                        dve.wait_ge(*at("vec", "lambda"))
                    r = stat(("rsum", i), 2)
                    c = 2 * (i % 4)
                    then(nc.vector.reciprocal(r, stat(("sum", "da", i // 4), 8)[:, c:c + 2]))
                    then(nc.vector.tensor_scalar(r[:, 1:2], r[:, 1:2], lam[:, 2:3], None, ALU.mult))
                    then(nc.vector.tensor_scalar(T[:, 256:512], T[:, 256:512], r[:, 1:2], None, ALU.mult))
                    signal(nc.vector.scalar_tensor_tensor(T[:, 0:256], T[:, 0:256], r[:, 0:1], T[:, 256:512],
                                                          ALU.mult, ALU.subtract), "vec", ("combined", i))
                elif kind == "da_norm":
                    qt, = a
                    dve.wait_ge(*at("act", ("da_sq", qt)))
                    signal(nc.vector.tensor_reduce(stat(("ss", ("da", qt)), 4),
                                                   ob1.rearrange("p (h d) -> p h d", h=4), AX.X, ALU.add),
                           "sumsq_vec", ("da", qt))
                elif kind == "da_heads":
                    qt, = a
                    dve.wait_ge(*at("rstd", ("da", qt)))
                    o = ob1.rearrange("p (h d) -> p h d", h=4)
                    signal(nc.vector.tensor_tensor(o, row[:, qt, 512:1024].rearrange("p (h d) -> p h d", h=4),
                                                   bcast(stat(("rstd", ("da", qt)), 4), P), ALU.mult),
                           "vec", ("heads", "da", qt), True)
                    signal(nc.vector.tensor_tensor(o, o, sub_w.rearrange("p (o d) -> p o d", o=1)
                                                   .to_broadcast([P, 4, P]), ALU.mult), "vec", ("y", "da", qt))
                elif kind == "head_norm":
                    kind, qt = a
                    dve.wait_ge(*at("pv_done", (kind, 4 * qt + 3)))
                    if kind == "na":
                        dve.wait_ge(*at("turned", ("y", "da", 1) if qt == 0 else ("y", "na", 0)))
                    r = stat(("sum", kind, qt), 8)
                    then(nc.vector.reciprocal(r, r))
                    o = ob1[:, :] if kind == "na" else ob2[:, qt, :]
                    i = nc.vector.tensor_tensor(o.rearrange("p (h d) -> p h d", h=8),
                                                aux[3].rearrange("p (h d) -> p h d", h=8), bcast(r, HD), ALU.mult)
                    i.then_inc(*tick("vec", ("heads", kind, qt)))
                    marks["vec", ("y", kind, qt)] = counts["vec"]
                elif kind == "turn_y":
                    kind, t = a
                    turned_low(("y", kind, t), 2, 4, yT, {"da": 0, "na": 4, "mla": 0, "gla": 4}[kind], t)
                elif kind == "ffn_turn":
                    name, t = a
                    j = int(name[-1])
                    n = SC[name][3][0][2] // P
                    f = (yT, 4 * j) if j < 2 else (fT, 4 * j - KD)
                    turned_low((name, t), (2 * j + t) % 4, n, f[0], f[1], t)
                elif kind == "latent_turn":
                    t, = a
                    turned_low(("latent", t, 0), 2 * t, 4, yT, 0, t)
                    turned_low(("latent", t, 1), 2 * t + 1, 1, yT, 4, t)
                elif kind == "decay_logits":
                    dve.wait_ge(*at("gla_done", "logits"))
                    signal(nc.vector.tensor_tensor(gl[:, :, :], aux[0][:, :].rearrange("p (t f) -> p t f", t=2),
                                                   gb_w.rearrange("p (o d) -> p o d", o=1).to_broadcast([P, 2, 256]),
                                                   ALU.add), "vec", "z", True)
                    signal(nc.vector.scalar_tensor_tensor(gz[:, :, :], gl[:, :, :], -1.0, gl[:, :, :],
                                                          ALU.mult, ALU.max), "vec", "abs_z")
                    dve.wait_ge(*at("act", "ln"))
                    signal(nc.vector.scalar_tensor_tensor(gl[:, :, :], gl[:, :, :], 0.0, gz[:, :, :],
                                                          ALU.min, ALU.subtract), "vec", "log_decay")
                elif kind == "gla_decay":
                    n, = a
                    m = LEVELS[n]
                    if n == 0:
                        dve.wait_ge(*at("act", "bT"))
                    else:
                        dve.wait_ge(*at("pool", ("level_q", n - 1)))
                        dve.wait_ge(*at("vec", ("level_k", n - 1)))
                    b = bT.rearrange("p f (b s) -> p (f b) s", s=2 * m)
                    e = ED.rearrange("p (b s) -> p b s", s=2 * m)
                    ref = b[:, :, m - 1:m].to_broadcast([P, 512 // (2 * m), m])
                    nc.vector.tensor_tensor(e[:, :, 0:m], ref, b[:, :, 0:m], ALU.subtract)\
                        .then_inc(*tick("vec", ("level_diff", n)))
                    nc.vector.tensor_tensor(e[:, :, m:2 * m], b[:, :, m:2 * m], ref, ALU.subtract)\
                        .then_inc(*tick("vec", ("level_diff", n)))
                elif kind == "gla_keys":
                    n, = a
                    dve.wait_ge(*at("act", ("level_exp", n)))
                    dve.wait_ge(*at("gla_done", ("level", n) if n else "sums"))
                    signal(nc.vector.tensor_tensor(KE[:, :, :].rearrange("p a b -> p (a b)"),
                                                   gkT.rearrange("p a b -> p (a b)"), ED[:, :], ALU.mult),
                           "vec", ("level_k", n))
                elif kind == "gla_level":
                    n, = a
                    dve.wait_ge(*at("gla_done", ("level", n)))
                    if n == 0:
                        dve.wait_ge(*at("pool", "attn_zero"))
                        dve.wait_ge(*at("pool", "level_masks"))
                    else:
                        dve.wait_ge(*at("vec", ("level", n - 1)))
                    for hb in range(2):
                        i = nc.vector.copy_predicated(
                            AC[:, hb, :, :],
                            lmask[:, n, :].bitcast(U32).rearrange("p (o j) -> p o j", o=1)
                            .to_broadcast([P, 4, GLA_CHUNK]),
                            aux[2 * (n % 2) + hb][:, 0:256].rearrange("p (k i) -> p k i", k=4))
                        i.then_inc(*tick("vec", ("level", n)))
                elif kind == "gla_state":
                    dve.wait_ge(*at("gla_done", "state"))
                    dve.wait_ge(*at("act", "dchunk"))
                    then(nc.vector.tensor_copy(ST[:, 0, :, :].rearrange("p f e -> p (f e)"), aux[2][:, 0:256]))
                    for c, b, col in ((1, 3, 0), (2, 2, 256)):
                        for f in range(2):
                            i = nc.vector.scalar_tensor_tensor(
                                ST[:, c, f, :], ST[:, c - 1, f, :], dchunk[:, f, c:c + 1],
                                aux[b][:, col + f * P:col + f * P + P], ALU.mult, ALU.add)
                            signal(i, "vec", "states", c == 1)
                elif kind == "gla_output":
                    t, = a
                    dve.wait_ge(*at("act", ("gla_sq", t)))
                    o = ob2[:, t, :].rearrange("p (h d) -> p h d", h=4)
                    signal(nc.vector.tensor_reduce(stat(("ss", ("gla", t)), 4), o, AX.X, ALU.add),
                           "sumsq_vec", ("gla", t))
                    dve.wait_ge(*at("rstd", ("gla", t)))
                    signal(nc.vector.tensor_tensor(o, aux[t].rearrange("p (h d) -> p h d", h=4),
                                                   bcast(stat(("rstd", ("gla", t)), 4), P), ALU.mult),
                           "vec", ("gla_heads", t))

            def setup():
                for i in range(16):
                    m = nc.vector.memset(inv[:, i:i + 1], 1.0 / (10000.0 ** (i / 16)))
                for n in range(4):
                    m = nc.vector.memset(stat("q_scale", 4)[:, n:n + 1], -HD ** -0.5 * 4.0 ** (n + 1))
                then(m)
                dve.wait_ge(*at("small_loaded", "positions"))
                then(nc.vector.tensor_copy(pos_f[:, :], pos_i[:, :]))
                for t in range(TOKS):
                    m = nc.vector.tensor_scalar(angle[:, t, :], inv[:, :], pos_f[:, t:t + 1], None, ALU.mult)
                then(m)
                magic = 1.5 * 2.0 ** 23
                then(nc.vector.tensor_scalar(turns[:, :, :], angle[:, :, :], 1 / (2 * math.pi), magic, ALU.mult, ALU.add))
                then(nc.vector.tensor_scalar(turns[:, :, :], turns[:, :, :], -magic, None, ALU.add))
                c1, c2 = 6.28125, 0.0019350051879882812
                c3 = 2 * math.pi - c1 - c2
                then(nc.vector.scalar_tensor_tensor(sin[:, :, :], turns[:, :, :], -c1, angle[:, :, :], ALU.mult, ALU.add))
                then(nc.vector.scalar_tensor_tensor(sin[:, :, :], turns[:, :, :], -c2, sin[:, :, :], ALU.mult, ALU.add))
                then(nc.vector.scalar_tensor_tensor(sin[:, :, :], turns[:, :, :], -c3, sin[:, :, :], ALU.mult, ALU.add))
                then(nc.vector.tensor_scalar(sin[:, :, :], sin[:, :, :], math.pi - 1e-6, -math.pi + 1e-6,
                                             ALU.min, ALU.max))
                then(nc.vector.scalar_tensor_tensor(angle[:, :, :], sin[:, :, :], -1.0, sin[:, :, :], ALU.mult, ALU.max))
                signal(nc.vector.tensor_scalar(angle[:, :, :], angle[:, :, :], -1.0, math.pi / 2, ALU.mult, ALU.add),
                       "vec", "sin_args")
                for n in range(2):
                    m = nc.vector.tensor_tensor_reduce(out=lam_in[:, 2 * n, :], in0=lam_in[:, 2 * n, :],
                                                       in1=lam_in[:, 2 * n + 1, :], scale=1.0, scalar=0.0, op0=ALU.mult,
                                                       op1=ALU.add, accum_out=lam[:, n:n + 1])
                    signal(m, "vec", "lambda_dots")
                nc.vector.tensor_scalar(sub_w[:, :], sub_w[:, :], 0.8, None, ALU.mult)
                dve.wait_ge(*at("pool", "iota"))
                nc.vector.scalar_tensor_tensor(dist[:, :, :], dist[:, :, :], -1.0, dist[:, :, :], ALU.mult, ALU.max)
                dve.wait_ge(*at("act", "lambda_exp"))
                then(nc.vector.tensor_tensor(lam[:, 2:3], lam[:, 0:1], lam[:, 1:2], ALU.subtract))
                signal(nc.vector.tensor_scalar(lam[:, 2:3], lam[:, 2:3], 0.8 - 0.6, None, ALU.add), "vec", "lambda", True)

            for i, st in enumerate(steps):
                if st[0] == "mm":
                    advance(ahead_of(i))
                elif st[0] == "take":
                    take(*st[1:])
                elif st[0] == "ahead":
                    advance(st[1])
                else:
                    step(*st[1:])

        @block.gpsimd
        def _(pool):
            g = nc.gpsimd

            def then(i):
                i.then_inc(*tick("pool_chain"))
                pool.wait_ge(*last_of("pool_chain"))

            def done(i, name, key):
                i.then_inc(*tick(name, key))
                pool.wait_ge(*last_of(name))

            def rstd(sem, key, n, width=1):
                pool.wait_ge(*at(sem, key))
                ms = stat(("ms", key), width)
                then(g.tensor_scalar(ms, stat(("ss", key), width), 1.0 / n, EPS, ALU.mult, ALU.add))
                done(g.tensor_tensor(stat(("rstd", key), width), ms, half[:, 0:width], ALU.pow), "rstd", key)

            def take(name, t):
                if name in ("out", "down"):
                    rstd("sumsq", ("post_" + name, t), D)
                elif name == "latent":
                    rstd("sumsq", ("cq", t), Q_RANK)
                    rstd("sumsq", ("ckv", t), KV_RANK)
                elif name == "gla_og":
                    pool.wait_ge(*at("acc_vec", (name, t)))
                    pool.wait_ge(*at("vec", "gln"))
                    s = sil[:, t, :].rearrange("p (h d) -> p h d", h=4)
                    done(g.tensor_tensor(s, s, gln_w.rearrange("p (o d) -> p o d", o=1).to_broadcast([P, 4, GLA_DV]),
                                    ALU.mult), "pool", ("silu", t))
                nxt = {"out": "ffn", "down": "mix2", "out2": "ffn2", "down2": "final"}.get(name)
                if nxt and not (last == 1 and name == "down"):
                    rstd("sumsq", (nxt, t), D)

            def step(kind, *a):
                if kind == "da_norm":
                    rstd("sumsq_vec", ("da", a[0]), GLA_DV, 4)
                elif kind == "decay_logits":
                    pool.wait_ge(*at("act", "exp_abs_z"))
                    done(g.tensor_scalar(gz[:, :, :], gz[:, :, :], 1.0, 1.0, ALU.mult, ALU.add), "pool", "one_plus")
                elif kind == "decay_sums":
                    pool.wait_ge(*at("act", "qdec_exp"))
                    for hb in range(2):
                        s = slice(hb * 64, hb * 64 + 64)
                        done(g.tensor_tensor(qdec[s, hb, :, :], qdec[s, hb, :, :], gqT[s, :, :], ALU.mult), "pool", "qdec")
                    pool.wait_ge(*at("act", "kdec_exp"))
                    done(g.tensor_tensor(kdec[:, :, :], kdec[:, :, :], gqk[:, :, 256:512], ALU.mult), "pool", "kdec")
                elif kind == "gla_decay":
                    n, = a
                    pool.wait_ge(*at("act", ("level_exp", n)))
                    if n:
                        pool.wait_ge(*at("gla_done", ("level", n)))
                    e = ED.rearrange("p (f s) -> p f s", f=2)
                    done(g.tensor_tensor(QE[:, :, :], gqT[:, :, :], e, ALU.mult), "pool", ("level_q", n))
                elif kind == "gla_state":
                    pool.wait_ge(*at("vec", ("level", len(LEVELS))))
                    for c in range(2):
                        s = slice(c * 64, c * 64 + 64)
                        for hb in range(2):
                            done(g.tensor_copy(AT[s, :, :, hb, c, :].rearrange("p t f i -> p (t f) i"), AC[s, hb, :, :]), "pool", "attn_blocks")
                elif kind == "gla_output":
                    t, = a
                    rstd("sumsq_vec", ("gla", t), GLA_DV, 4)
                    pool.wait_ge(*at("vec", ("gla_heads", t)))
                    pool.wait_ge(*at("pool", ("silu", t)))
                    done(g.tensor_tensor(ob2[:, t, :], ob2[:, t, :], sil[:, t, :], ALU.mult), "pool", ("y", "gla", t))

            then(g.memset(half[:, :], -0.5))
            then(g.memset(ident[:, :], 0.0))
            done(g.affine_select(out=ident[:, :], in_=ident[:, :], compare_op=ALU.not_equal, fill=1.0, base=0,
                            pattern=[[-1, P]], channel_multiplier=1), "pool", "ident")
            for t in range(TOKS):
                rstd("sumsq", ("mix", t), D)
            done(g.iota(dist[:, :, :], pattern=[[-P, TOKS], [1, SEQ]], base=0, channel_multiplier=-1,
                   allow_small_or_imprecise_dtypes=True), "pool", "iota")
            pool.wait_ge(*at("normed", ("mix", 1)))
            for T in (qaT, qbT):
                for n in range(2):
                    done(g.memset(T[64 - 64 * n:128 - 64 * n, n, :, :], 0.0), "pool", "q_zero")
            pool.wait_ge(*at("bias_loaded", (1, NA_HEADS - 1)))
            flat = gates1.rearrange("p g t d -> p (g t d)")[:, 0:NA_HEADS * 6 * GRID]
            nb = nbias.rearrange("p h t j -> p (h t) j")
            then(g.tensor_scalar(nb, flat.rearrange("p (k j) -> p k j", j=GRID)[:, :, ::-1], -1.0, 0.0,
                                 ALU.mult, ALU.add))
            edge = NA_COLS // 2
            for r in range(2):
                s = slice(r * GRID, (r + 1) * GRID)
                part = nb[s, :, 0:GRID - NA_COLS]
                then(g.affine_select(out=part, in_=part, compare_op=ALU.is_ge, fill=FAR, base=edge,
                                     pattern=[[0, NA_HEADS * 6], [1, GRID - NA_COLS]], channel_multiplier=-1))
                part = nb[s, :, NA_COLS:GRID]
                done(g.affine_select(out=part, in_=part, compare_op=ALU.is_ge, fill=FAR, base=edge - 1 - NA_COLS,
                                     pattern=[[0, NA_HEADS * 6], [-1, GRID - NA_COLS]], channel_multiplier=1),
                     "pool", "bias_masked")
            then(g.memset(causal[:, :], 0.0))
            done(g.affine_select(out=causal[:, P:SEQ], in_=causal[:, P:SEQ], compare_op=ALU.is_ge, fill=FAR, base=0,
                            pattern=[[-1, P]], channel_multiplier=1), "pool", "causal")
            then(g.memset(upto[:, :], 1.0 / 16.0))
            then(g.memset(after[:, :], 1.0 / 16.0))
            then(g.affine_select(out=upto[:, :], in_=upto[:, :], compare_op=ALU.is_ge, fill=0.0, base=0,
                                 pattern=[[1, P]], channel_multiplier=-1))
            then(g.affine_select(out=after[:, :], in_=after[:, :], compare_op=ALU.is_ge, fill=0.0, base=-1,
                                 pattern=[[-1, P]], channel_multiplier=1))
            then(g.memset(upto[0:64, 64:128], 0.0))
            done(g.memset(after[64:128, 0:64], 0.0), "pool", "sum_masks")
            then(g.memset(lmask[:, :, :], 0.0))
            for r in range(2):
                s = slice(64 * r, 64 * r + 64)
                then(g.affine_select(out=lmask[s, 0, :], in_=lmask[s, 0, :], compare_op=ALU.not_equal, fill=1.0,
                                     base=0, pattern=[[-1, 64]], channel_multiplier=1))
            for n, m in enumerate(LEVELS):
                part = lmask[:, n + 1, :].rearrange("p (b s) -> p b s", s=2 * m)[:, :, m:2 * m]
                then(g.memset(part, 1.0))
                for r in range(2):
                    q = part[64 * r:64 * r + 64]
                    then(g.affine_select(out=q, in_=q, compare_op=ALU.is_ge, fill=0.0, base=0,
                                         pattern=[[-2 * m, 32 // m], [0, m]], channel_multiplier=1))
                    then(g.affine_select(out=q, in_=q, compare_op=ALU.is_ge, fill=0.0, base=m - 1,
                                         pattern=[[2 * m, 32 // m], [0, m]], channel_multiplier=-1))
            done(g.memset(half[:, :], -0.5), "pool", "level_masks")
            for i, st in enumerate(steps):
                if st == ("do", "gla_qk_turn", 0):
                    pool.wait_ge(*at("mm_done", ("latent", 1)))
                    for n in range(2):
                        then(g.memset(qdec[64 - 64 * n:128 - 64 * n, n, :, :], 0.0))
                    then(g.memset(AT[:, :, :, :, :, :].rearrange("p a b c d e -> p (a b c d e)"), 0.0))
                    done(g.memset(AC[:, :, :, :].rearrange("p a b c -> p (a b c)"), 0.0), "pool", "attn_zero")
                if st[0] == "take":
                    take(*st[1:])
                elif st[0] in ("mm", "ahead"):
                    continue
                else:
                    step(*st[1:])

    return marks


_INS = ['x', 'pre_mix_w', 'w_in', 'b_gate', 'lambda_q1', 'lambda_k1', 'lambda_q2', 'lambda_k2', 'subln_w', 'rpb',
        'w_branch_a', 'w_branch_b', 'w_out', 'post_mix_w', 'pre_ffn_w', 'w_gate', 'w_up', 'w_down', 'post_ffn_w',
        'positions_2', 'ln_mix_2', 'w_in_2', 'mla_norm_cq_2', 'mla_w_uq_2', 'mla_norm_ckv_2', 'mla_w_ukv_2',
        'mla_w_o_2', 'gla_w_gate2_2', 'gla_b_gate_2', 'gla_norm_2', 'gla_w_o_2', 'w_out_2', 'ln_ffn_2',
        'ffn_w_gate_2', 'ffn_w_up_2', 'ffn_w_down_2', 'final_norm_2']
LAST = 2


def kernel(**inputs):
    import numpy as _np
    import concourse.bacc as _bacc
    from concourse import mybir as _mybir
    from concourse.bass_utils import run_bass_kernel_spmd as _run

    known = None
    for _ in range(2):
        nc = _bacc.Bacc("TRN2", target_bir_lowering=False, num_devices=1)
        arrays, args = {}, {}
        for name in _INS:
            a = inputs[name]
            if name == 'rpb':
                a = a[..., ::-1]
            a = _np.ascontiguousarray(a)
            arrays[f"in_{name}_dram"] = a
            args[name] = nc.dram_tensor(f"in_{name}_dram", a.shape, _mybir.dt.from_np(a.dtype),
                                        kind="ExternalInput").ap()
        out = nc.dram_tensor("out_0_dram", (1, SEQ, D), _mybir.dt.float32, kind="ExternalOutput").ap()
        known = program(nc, known, LAST, args, out)
    r = _run(nc, [arrays], core_ids=[0])
    return r.results[0]["out_0_dram"]
```
